# Optimizing a Trainium2 kernel written in Bass

```python
import math
import jax, jax.numpy as jnp
from jax import lax
import numpy as np

D_MODEL = 1024
BATCH = 1
SEQ = 1024
DEPTH = 1
DEC_BATCH = 8
DEC_SEQ = 16
PAST_LEN = 256

CHUNK = 64
HEAD_DIM = 64
D_MIX = D_MODEL
D_FOX = D_MIX // 4
H_FOX = D_FOX // HEAD_DIM
D_BAND = D_MIX // 4
H_BAND = D_BAND // HEAD_DIM
D_LRU = D_MIX // 2
LRU_BLOCKS = 8
LRU_BW = D_LRU // LRU_BLOCKS
LRU_CONV = 4
RGLRU_C = 8.0
BAND_PREV = 8
BAND_LEN = (BAND_PREV + 1) * CHUNK
BAND_KEEP = BAND_PREV * CHUNK
REL_CLIP = 128
N_REL = REL_CLIP + CHUNK
D_FF = 3 * D_MODEL
FFN_CONV = 3
FOX_QBLOCK = 128
RMS_EPS = 1e-6
NEG_INF = -1e30
ATTN_SCALE = HEAD_DIM ** -0.5
SPLIT_SIZES = (D_FOX, D_FOX, D_FOX, H_FOX, D_LRU, D_LRU, D_BAND, D_BAND, D_BAND)
N_IN = 3 * D_FOX + H_FOX + 2 * D_LRU + 3 * D_BAND

kernel_name = 'hybrid_streaming_encoder_step'

def rms_norm(x, g):
    xf = x.astype(jnp.float32)
    y = xf * lax.rsqrt(jnp.mean(xf * xf, axis=-1, keepdims=True) + RMS_EPS)
    return (y * g.astype(jnp.float32)).astype(x.dtype)

def causal_dwconv(x, hist, w, b):
    T = x.shape[1]
    width = w.shape[0]
    xp = jnp.concatenate([hist, x], axis=1)
    y = xp[:, 0:T] * w[0]
    for k in range(1, width):
        y = y + xp[:, k:k + T] * w[k]
    return y + b, xp[:, xp.shape[1] - (width - 1):]

def fox_attention(q, k_all, v_all, logf_all, n_hist):
    B, T, H, D = q.shape
    S = k_all.shape[1]
    qb = min(FOX_QBLOCK, T)
    nb = T // qb
    c = jnp.cumsum(logf_all.astype(jnp.float32), axis=1).transpose(0, 2, 1)
    q_blocks = q.reshape(B, nb, qb, H, D).transpose(1, 0, 2, 3, 4)
    c_q = c[:, :, n_hist:].reshape(B, H, nb, qb).transpose(2, 0, 1, 3)
    k_pos = jnp.arange(S)

    def one_block(args):
        q_blk, cq_blk, blk = args
        s = jnp.einsum('bqhd,bkhd->bhqk', q_blk, k_all, preferred_element_type=jnp.float32) * ATTN_SCALE
        s = s + cq_blk[..., None] - c[:, :, None, :]
        q_pos = n_hist + blk * qb + jnp.arange(qb)
        s = jnp.where(k_pos[None, :] <= q_pos[:, None], s, NEG_INF)
        p = jax.nn.softmax(s, axis=-1).astype(v_all.dtype)
        return jnp.einsum('bhqk,bkhd->bqhd', p, v_all)

    out = lax.map(one_block, (q_blocks, c_q, jnp.arange(nb)))
    return out.transpose(1, 0, 2, 3, 4).reshape(B, T, H, D)

def band_attention(q, k_all, v_all, n_hist, rel_table):
    B, T, H, D = q.shape
    nq = -(-T // CHUNK)
    tq = nq * CHUNK
    front = BAND_KEEP - n_hist
    pad = ((0, 0), (front, tq - T), (0, 0), (0, 0))
    n_kc = BAND_PREV + nq
    k_ch = jnp.pad(k_all, pad).reshape(B, n_kc, CHUNK, H, D)
    v_ch = jnp.pad(v_all, pad).reshape(B, n_kc, CHUNK, H, D)
    gidx = jnp.arange(nq)[:, None] + jnp.arange(BAND_PREV + 1)[None, :]
    k_band = k_ch[:, gidx].reshape(B, nq, BAND_LEN, H, D)
    v_band = v_ch[:, gidx].reshape(B, nq, BAND_LEN, H, D)
    q_ch = jnp.pad(q, ((0, 0), (0, tq - T), (0, 0), (0, 0))).reshape(B, nq, CHUNK, H, D)
    s = jnp.einsum('bnqhd,bnkhd->bnhqk', q_ch, k_band, preferred_element_type=jnp.float32) * ATTN_SCALE
    i = jnp.arange(CHUNK)
    j = jnp.arange(BAND_LEN)
    dist = j[None, :] - BAND_KEEP - i[:, None]
    ridx = jnp.clip(dist, -REL_CLIP, CHUNK - 1) + REL_CLIP
    bias = rel_table[:, ridx].astype(jnp.float32)
    gpos = jnp.arange(nq)[:, None] * CHUNK + j[None, :]
    valid = (gpos >= front) & (gpos < front + n_hist + T)
    s = jnp.where(valid[None, :, None, None, :], s + bias[None, None], NEG_INF)
    p = jax.nn.softmax(s, axis=-1).astype(v_all.dtype)
    o = jnp.einsum('bnhqk,bnkhd->bnqhd', p, v_band)
    return o.reshape(B, tq, H, D)[:, :T]

def _linear_combine(e1, e2):
    a1, b1 = e1
    a2, b2 = e2
    return a1 * a2, a2 * b1 + b2

def rglru_block(xb, yb, conv_hist, h0, conv_w, conv_b, w_a, b_a, w_x, b_x, lam):
    B, T, C = xb.shape
    xc, conv_new = causal_dwconv(xb, conv_hist, conv_w, conv_b)
    xg = xc.reshape(B, T, LRU_BLOCKS, LRU_BW)
    r = jax.nn.sigmoid((jnp.einsum('btnd,nde->btne', xg, w_a).reshape(B, T, C) + b_a).astype(jnp.float32))
    ig = jax.nn.sigmoid((jnp.einsum('btnd,nde->btne', xg, w_x).reshape(B, T, C) + b_x).astype(jnp.float32))
    log_a = RGLRU_C * r * jax.nn.log_sigmoid(lam.astype(jnp.float32))
    a = jnp.exp(log_a)
    u = jnp.sqrt(-jnp.expm1(2.0 * log_a)) * (ig * xc.astype(jnp.float32))
    a_cum, h_part = lax.associative_scan(_linear_combine, (a, u), axis=1)
    h = a_cum * h0.astype(jnp.float32)[:, None, :] + h_part
    y = h.astype(xb.dtype) * jax.nn.gelu(yb)
    return y, h[:, -1].astype(xb.dtype), conv_new

def trunk_layer(x, fox_k_h, fox_v_h, fox_lf_h, band_k_h, band_v_h, lru_h0, lru_conv_h, ffn_conv_h,
                norm_g, w_in, b_forget, lru_conv_w, lru_conv_b, lru_wa, lru_ba, lru_wx, lru_bx,
                lru_lambda, rel_bias, w_out, w_up, ffn_conv_w, ffn_conv_b, w_down):
    B, T, _ = x.shape
    split_points = np.cumsum(SPLIT_SIZES)[:-1].tolist()
    h = rms_norm(x, norm_g[0])
    qa, ka, va, fa, xb, yb, qc, kc, vc = jnp.split(h @ w_in, split_points, axis=-1)
    qa = qa.reshape(B, T, H_FOX, HEAD_DIM)
    ka = ka.reshape(B, T, H_FOX, HEAD_DIM)
    va = va.reshape(B, T, H_FOX, HEAD_DIM)
    qc = qc.reshape(B, T, H_BAND, HEAD_DIM)
    kc = kc.reshape(B, T, H_BAND, HEAD_DIM)
    vc = vc.reshape(B, T, H_BAND, HEAD_DIM)
    logf = jax.nn.log_sigmoid(fa.astype(jnp.float32) + b_forget.astype(jnp.float32)).astype(x.dtype)

    o_fox = fox_attention(qa, jnp.concatenate([fox_k_h, ka], axis=1), jnp.concatenate([fox_v_h, va], axis=1),
                          jnp.concatenate([fox_lf_h, logf], axis=1), fox_k_h.shape[1])
    o_lru, h_last, lru_conv_new = rglru_block(xb, yb, lru_conv_h, lru_h0, lru_conv_w, lru_conv_b,
                                              lru_wa, lru_ba, lru_wx, lru_bx, lru_lambda)
    o_band = band_attention(qc, jnp.concatenate([band_k_h, kc], axis=1), jnp.concatenate([band_v_h, vc], axis=1),
                            band_k_h.shape[1], rel_bias)
    mix = jnp.concatenate([o_fox.reshape(B, T, D_FOX), o_lru, o_band.reshape(B, T, D_BAND)], axis=-1) @ w_out
    x = x + rms_norm(mix, norm_g[1])

    h2 = rms_norm(x, norm_g[2])
    gate, val = jnp.split(h2 @ w_up, 2, axis=-1)
    gate_c, ffn_conv_new = causal_dwconv(gate, ffn_conv_h, ffn_conv_w, ffn_conv_b)
    f = (jax.nn.gelu(gate_c) * val) @ w_down
    x = x + rms_norm(f, norm_g[3])

    keep = min(BAND_KEEP, T)
    return x, (ka, va, logf, kc[:, T - keep:], vc[:, T - keep:], h_last, lru_conv_new, ffn_conv_new)

def setup_inputs(seed: int = 0) -> dict:
    key = jax.random.key(seed)
    ks = jax.random.split(key, 26)
    f32 = jnp.float32

    def nrm(k, shape, scale):
        return jax.random.normal(k, shape, f32) * scale

    band_past = min(BAND_KEEP, PAST_LEN)
    u = jax.random.uniform(ks[19], (DEPTH, D_LRU), f32, 0.9, 0.999)
    s = u ** (1.0 / RGLRU_C)
    lam = jnp.log(s) - jnp.log1p(-s)
    return {
        'x_prompt': nrm(ks[0], (BATCH, SEQ, D_MODEL), 1.0),
        'x_sample': nrm(ks[1], (DEC_BATCH, DEC_SEQ, D_MODEL), 1.0),
        'cache_fox_k': nrm(ks[2], (DEPTH, DEC_BATCH, PAST_LEN, H_FOX, HEAD_DIM), 1.0),
        'cache_fox_v': nrm(ks[3], (DEPTH, DEC_BATCH, PAST_LEN, H_FOX, HEAD_DIM), 1.0),
        'cache_fox_logf': jax.nn.log_sigmoid(2.5 + nrm(ks[4], (DEPTH, DEC_BATCH, PAST_LEN, H_FOX), 1.0)),
        'cache_band_k': nrm(ks[5], (DEPTH, DEC_BATCH, band_past, H_BAND, HEAD_DIM), 1.0),
        'cache_band_v': nrm(ks[6], (DEPTH, DEC_BATCH, band_past, H_BAND, HEAD_DIM), 1.0),
        'state_lru_h': nrm(ks[7], (DEPTH, DEC_BATCH, D_LRU), 0.5),
        'state_lru_conv': nrm(ks[8], (DEPTH, DEC_BATCH, LRU_CONV - 1, D_LRU), 1.0),
        'state_ffn_conv': nrm(ks[9], (DEPTH, DEC_BATCH, FFN_CONV - 1, D_FF), 1.0),
        'norm_g': 1.0 + nrm(ks[10], (DEPTH, 4, D_MODEL), 0.05),
        'w_in': nrm(ks[11], (DEPTH, D_MODEL, N_IN), D_MODEL ** -0.5),
        'b_forget': jax.random.uniform(ks[12], (DEPTH, H_FOX), f32, 1.0, 4.0),
        'lru_conv_w': nrm(ks[13], (DEPTH, LRU_CONV, D_LRU), LRU_CONV ** -0.5),
        'lru_conv_b': nrm(ks[14], (DEPTH, D_LRU), 0.01),
        'lru_wa': nrm(ks[15], (DEPTH, LRU_BLOCKS, LRU_BW, LRU_BW), LRU_BW ** -0.5),
        'lru_ba': nrm(ks[16], (DEPTH, D_LRU), 0.01),
        'lru_wx': nrm(ks[17], (DEPTH, LRU_BLOCKS, LRU_BW, LRU_BW), LRU_BW ** -0.5),
        'lru_bx': nrm(ks[18], (DEPTH, D_LRU), 0.01),
        'lru_lambda': lam,
        'rel_bias': nrm(ks[20], (DEPTH, H_BAND, N_REL), 0.2),
        'w_out': nrm(ks[21], (DEPTH, D_MIX, D_MODEL), D_MIX ** -0.5),
        'w_up': nrm(ks[22], (DEPTH, D_MODEL, 2 * D_FF), D_MODEL ** -0.5),
        'ffn_conv_w': nrm(ks[23], (DEPTH, FFN_CONV, D_FF), FFN_CONV ** -0.5),
        'ffn_conv_b': nrm(ks[24], (DEPTH, D_FF), 0.01),
        'w_down': nrm(ks[25], (DEPTH, D_FF, D_MODEL), D_FF ** -0.5),
    }

def reference(x_prompt, x_sample, cache_fox_k, cache_fox_v, cache_fox_logf, cache_band_k, cache_band_v,
              state_lru_h, state_lru_conv, state_ffn_conv, norm_g, w_in, b_forget, lru_conv_w, lru_conv_b,
              lru_wa, lru_ba, lru_wx, lru_bx, lru_lambda, rel_bias, w_out, w_up, ffn_conv_w, ffn_conv_b, w_down):
    dt = x_prompt.dtype
    bp = x_prompt.shape[0]
    prompt_hist = (
        jnp.zeros((bp, 0, H_FOX, HEAD_DIM), dt),
        jnp.zeros((bp, 0, H_FOX, HEAD_DIM), dt),
        jnp.zeros((bp, 0, H_FOX), dt),
        jnp.zeros((bp, 0, H_BAND, HEAD_DIM), dt),
        jnp.zeros((bp, 0, H_BAND, HEAD_DIM), dt),
        jnp.zeros((bp, D_LRU), dt),
        jnp.zeros((bp, LRU_CONV - 1, D_LRU), dt),
        jnp.zeros((bp, FFN_CONV - 1, D_FF), dt),
    )
    xp, xs = x_prompt, x_sample
    st_p, st_s = [], []
    for l in range(DEPTH):
        params = (norm_g[l], w_in[l], b_forget[l], lru_conv_w[l], lru_conv_b[l], lru_wa[l], lru_ba[l],
                  lru_wx[l], lru_bx[l], lru_lambda[l], rel_bias[l], w_out[l], w_up[l], ffn_conv_w[l],
                  ffn_conv_b[l], w_down[l])
        sample_hist = (cache_fox_k[l], cache_fox_v[l], cache_fox_logf[l], cache_band_k[l], cache_band_v[l],
                       state_lru_h[l], state_lru_conv[l], state_ffn_conv[l])
        xp, new_p = trunk_layer(xp, *prompt_hist, *params)
        xs, new_s = trunk_layer(xs, *sample_hist, *params)
        st_p.append(new_p)
        st_s.append(new_s)

    def stack(states, j):
        return jnp.stack([st[j] for st in states], axis=0)

    fox_k_p, fox_k_s = stack(st_p, 0), stack(st_s, 0)
    fox_v_p, fox_v_s = stack(st_p, 1), stack(st_s, 1)
    fox_logf_p, fox_logf_s = stack(st_p, 2), stack(st_s, 2)
    band_k_p, band_k_s = stack(st_p, 3), stack(st_s, 3)
    band_v_p, band_v_s = stack(st_p, 4), stack(st_s, 4)
    lru_h_p, lru_h_s = stack(st_p, 5), stack(st_s, 5)
    lru_conv_p, lru_conv_s = stack(st_p, 6), stack(st_s, 6)
    ffn_conv_p, ffn_conv_s = stack(st_p, 7), stack(st_s, 7)
    return (xp, xs, fox_k_p, fox_k_s, fox_v_p, fox_v_s, fox_logf_p, fox_logf_s, band_k_p, band_k_s,
            band_v_p, band_v_s, lru_h_p, lru_h_s, lru_conv_p, lru_conv_s, ffn_conv_p, ffn_conv_s)


_drawn_inputs = setup_inputs


def setup_inputs(seed=0):
    import zlib

    import numpy as np

    out = dict(_drawn_inputs(seed))
    spreads = {}
    factors = {'lru_ba': 22.322, 'lru_bx': 21.695, 'ffn_conv_b': 8.0}
    for name, (base, spread) in spreads.items():
        noise = np.random.default_rng([zlib.crc32(name.encode()), seed]).standard_normal(out[name].shape)
        drawn = base * np.exp(spread * noise) if base else spread * noise
        out[name] = __import__('jax').numpy.asarray(drawn.astype(out[name].dtype))
    for name, factor in factors.items():
        out[name] = (out[name] * factor).astype(out[name].dtype)
    return out
```

```python
from contextlib import ExitStack

import concourse.bass as bass
from concourse import mybir

F32 = mybir.dt.float32
F32R = mybir.dt.float32r
BF16 = mybir.dt.bfloat16
ALU = mybir.AluOpType
ACT = mybir.ActivationFunctionType
AX = mybir.AxisListType

P = 128
D = 1024
KD = D // P
SEQ = 1024
NPT = SEQ // P
NS, TS = 8, 16
T = SEQ + NS * TS
NT = T // P
CW = T // 3
PAST = 256
CHUNK, HD = 64, 64
H = 4
DH = H * HD
DL = 512
LT = DL // P
LCONV, FCONV = 4, 3
DFF = 3072
FT = DFF // P
FG = 2
NG = FT // FG
NREL = 192
BANDW = 640
EPS = 1e-6
QS = -(HD ** -0.5)
BIG = 1e30
START = 3e38
SK = PAST + TS

LH = LCONV - 1
LPAD = LH + SEQ + NS * (LH + TS)
LW = LPAD - LH
FH = FCONV - 1
FPAD = FH + SEQ + NS * (FH + TS)
FW = FPAD - FH

C_FQ, C_FK, C_FV, C_FA = 0, DH, 2 * DH, 3 * DH
C_X = 3 * DH + H
C_Y = C_X + DL
C_BQ = C_Y + DL
C_BK, C_BV = C_BQ + DH, C_BQ + 2 * DH

UNITS = [("x", C_X), ("x", C_X + 256), ("y", C_Y), ("y", C_Y + 256), ("fk", C_FK), ("fv", C_FV),
         ("bk", C_BK), ("bv", C_BV), ("fq", C_FQ), ("bq", C_BQ)]
KV = ("fk", "fv", "bk", "bv")
NU = len(UNITS)
MIX_OF_X = [0, 1, 6, 7]


def projection_outputs():
    outs = []
    for u, (kind, _) in enumerate(UNITS):
        first = {"x": 2 * u, "y": 2 * (u - 2)}.get(kind, 0)
        outs += [(kind, u, first + c) for c in range(3 if kind in KV else 2)]
        if 2 <= u <= 5:
            outs += [("gate_r", None, u - 2), ("gate_i", None, u - 2)]
    return outs + [("fa", None, 0)]


OUTS = projection_outputs()
NO = len(OUTS)


KV_OUTS = [n for n, out in enumerate(OUTS) if out[0] in KV]


def last_output(u):
    return max(n for n, o in enumerate(OUTS) if o[1] == u)


def attention_steps():
    steps = [("pf", h, i) for i in range(NPT) for h in range(H)]
    steps += [("sf", p) for p in range(NS // 2)]
    steps += [("pb", h, i) for i in range(NPT) for h in range(H)]
    steps += [("sb", p) for p in range(NS // 2)]
    return steps


STEPS = attention_steps()
NSTEP = len(STEPS)


def key_blocks(step):
    if step[0] == "pf":
        return 0, step[2] + 1
    first = max(0, step[2] - 4)
    return first, step[2] - first + 1


def stage_stores():
    lots = []
    for kind in KV:
        for tg in range(3):
            t0 = 3 * tg
            np_ = 3 if tg < 2 else 2
            if kind[0] == "f":
                lot = [(kind + "_p", t0, np_, 0)]
            else:
                lot = [(kind + "_scr", t0, 3, 0)]
                if tg == 1:
                    lot.append((kind + "_p", 4, 2, 1))
                if tg == 2:
                    lot.append((kind + "_p", 6, 2, 0))
            if tg == 2:
                lot.append((kind + "_s", 8, 1, 2))
            lots.append(lot)
    return lots


STORES = stage_stores()


def stores_until(slot, s):
    return sum(len(STORES[q]) for q in range(s + 1) if q % 2 == slot)


def bank_of(q):
    return (6 + q) % 8


class Chain:

    def __init__(self, eng, sem):
        self.eng, self.sem, self.base, self.n = eng, sem, 0, 0

    def __call__(self, ins):
        self.n += 1
        ins.then_inc(self.sem, 1)
        self.eng.wait_ge(self.sem, self.base + self.n)


def encoder_step(nc, i, o):
    with ExitStack() as ctx:
        def sb(name, shape, dt=F32, stack=ctx):
            return stack.enter_context(nc.sbuf_tensor(name, shape, dt))

        def sem(name):
            return ctx.enter_context(nc.semaphore(name))

        ident = sb("ident", [P, P])
        ident_b = sb("ident_b", [P, P], BF16)
        cmask_b = sb("cmask_b", [P, P], BF16)
        chan = sb("chan", [P, 6, P])
        gains = sb("gains", [P, 2, D])
        lru_state = sb("lru_state", [P, LT, 36])
        stat = sb("stat", [P, 320])

        with ExitStack() as s:
            act_hi = sb("act_hi", [P, KD, T], F32R, s)
            act_lo = sb("act_lo", [P, KD, T], F32R, s)
        with ExitStack() as s:
            kt_f = sb("kt_f", [P, 2, T], F32, s)
            kt_b = sb("kt_b", [P, 2, T], F32, s)
            v_f = sb("v_f", [P, NT, DH], F32, s)
            v_b = sb("v_b", [P, NT, DH], F32, s)
            cum_b = sb("cum_b", [P, H, SEQ], F32, s)
            band_bias = sb("band_bias", [P, H, BANDW], F32, s)
            q_blocks = sb("q_blocks", [P, NS, 2, 64], F32, s)
            logf_rows = sb("logf_rows", [P, 2 * NS, 64], F32, s)
            logf_new = sb("logf_new", [P, NS, 64], F32, s)
        with ExitStack() as s:
            x1_back = sb("x1_back", [P, NT, D], F32, s)
            ffn_rows = sb("ffn_rows", [18, DFF], F32, s)
            square3 = sb("square3", [P, D], F32, s)
        sb("region_a", [P, 2 * KD * T])
        with ExitStack() as s:
            w_hi = sb("w_hi", [P, 3, 2048], F32R, s)
            w_lo = sb("w_lo", [P, 3, 2048], F32R, s)
        with ExitStack() as s:
            cache_k = sb("cache_k", [P, NS, 2, DH], F32, s)
            cache_v = sb("cache_v", [P, NS, 2, DH], F32, s)
            kt_s = sb("kt_s", [P, NS, 2, PAST], F32, s)
        sb("region_w", [P, 2 * 3 * 2048])
        raw = sb("raw", [P, 2, 1024])
        with ExitStack() as s:
            x_in = sb("x_in", [P, 3, D], F32, s)
            y_in = sb("y_in", [P, 2, D], F32, s)
            square0 = sb("square0", [P, D], F32, s)
            chan_rows = sb("chan_rows", [P, 6, P], F32, s)
        with ExitStack() as s:
            f_acc = sb("f_acc", [P, NT, D], F32, s)
            f_hi = sb("f_hi", [P, FG, T], F32R, s)
            f_lo = sb("f_lo", [P, FG, T], F32R, s)
            gate_pad = sb("gate_pad", [P, FPAD], F32, s)
            gate_conv = sb("gate_conv", [P, FW], F32, s)
            ffn_state = sb("ffn_state", [P, FT, 18], F32, s)
        mix = sb("mix", [P, KD, T])
        with ExitStack() as s:
            gate_w = sb("gate_w", [P, 2, LT, P], F32, s)
            xpad = sb("xpad", [P, LPAD], F32, s)
            xconv = sb("xconv", [P, LW], F32, s)
            gate_r = sb("gate_r", [P, LW], F32, s)
            gate_i = sb("gate_i", [P, LW], F32, s)
            stage = sb("stage", [P, 2, 3, DH], F32, s)
            fa_raw = sb("fa_raw", [P, KD, H], F32, s)
            fa_hi = sb("fa_hi", [P, KD, H], F32R, s)
            fa_lo = sb("fa_lo", [P, KD, H], F32R, s)
        with ExitStack() as s:
            probs = sb("probs", [P, 2, 1024], F32, s)
            probs_t = sb("probs_t", [P, 2, 1024], F32, s)
            k_rows = sb("k_rows", [P, NT, DH], F32, s)
            fox_mask_s = sb("fox_mask_s", [P, SK], F32, s)
            band_bias_s = sb("band_bias_s", [P, SK], F32, s)
            upper = sb("upper", [P, SK], F32, s)
            logf = sb("logf", [P, NT, H], F32, s)
            cache_logf = sb("cache_logf", [P, 2 * NS, H], F32, s)
        with ExitStack() as s:
            wx_hi = sb("wx_hi", [P, 2048], F32R, s)
            wx_lo = sb("wx_lo", [P, 2048], F32R, s)
            x_res = sb("x_res", [P, D], F32, s)
            x1 = sb("x1", [P, D], F32, s)
            y2 = sb("y2", [P, D], F32, s)
        fa_rows = probs_t[0:H, :, :].rearrange("p a b -> p (a b)")[:, 0:T]
        cum_rows = probs[0:H, 0, 0:SEQ]
        one_rows = probs[0:H, 1, 0:SEQ]
        rel_rows = k_rows[:, 0:6, :].rearrange("p a b -> p (a b)").rearrange("p (h c) -> p h c", h=H)
        state_rows = probs_t[:, 1, 512:1024]

        PS = ctx.enter_context(nc.psum_tensor("PS", [P, 8, 512], F32))

        x1_dram = nc.dram_tensor("x1_scratch", [T, D], F32, kind="Internal").ap()
        cum_dram = nc.dram_tensor("cum_scratch", [H, SEQ], F32, kind="Internal").ap()
        rel_dram = nc.dram_tensor("rel_scratch", [P, H * 384], F32, kind="Internal")
        kv_dram = {k + "_scr": nc.dram_tensor(k + "_scratch", [T, DH], F32, kind="Internal").ap() for k in ("bk", "bv")}
        kv_out = {}
        for kind, name in (("fk", "fox_k"), ("fv", "fox_v"), ("bk", "band_k"), ("bv", "band_v")):
            kv_out[kind + "_p"] = o[name + "_p"].rearrange("l b s h d -> (l b s) (h d)")
            kv_out[kind + "_s"] = o[name + "_s"].rearrange("l b s h d -> (l b s) (h d)")
        xp = i["x_prompt"].rearrange("b s d -> (b s) d")
        xs = i["x_sample"].rearrange("b s d -> (b s) d")
        yp = o["y_prompt"].rearrange("b s d -> (b s) d")
        ys = o["y_sample"].rearrange("b s d -> (b s) d")
        w_in = i["w_in"][0]
        w_out = i["w_out"][0]
        w_up = i["w_up"][0]
        w_down = i["w_down"][0]

        def rows_of(p_ap, s_ap, t):
            return p_ap[t * P:(t + 1) * P, :] if t < NPT else s_ap

        def tile_rows(ap, t0, n):
            return ap[t0 * P:(t0 + n) * P, :].rearrange("(c p) d -> p c d", p=P)

        def lru_const(k, j):
            return chan[:, 0, k * LT + j:k * LT + j + 1]
        lam = chan[:, 0, 7 * LT:8 * LT]
        h0 = chan[:, 0, 32:64].rearrange("p (b j) -> p b j", j=LT)
        lru_hist = chan[:, 2, 0:96].rearrange("p (b k j) -> p b k j", k=LH, j=LT)
        ffn_const = chan[:, 1, 0:96]
        ffn_hist = chan[:, 3:6, :].rearrange("p s c -> p (s c)").rearrange("p (b k j) -> p b k j", k=FH, j=FT)

        SS0, RM0, RR0 = 0, 9, 18
        SP4 = 28
        EPSC = 32
        RMIN, RSUM, RINV = 40, 42, 44
        SS1, SS2, SS3 = 48, 57, 66
        BF_ = 76
        BLK = 80
        TMP = 88

        chan_loaded = sem("chan_loaded")
        chan_turned = sem("chan_turned")
        chan_ready = sem("chan_ready")
        gain_loaded = sem("gain_loaded")
        gain2_loaded = sem("gain2_loaded")
        gain3_loaded = sem("gain3_loaded")
        consts_ready = sem("consts_ready")
        pool_step = sem("pool_step")
        act_step = sem("act_step")
        dve_step = sem("dve_step")
        x_loaded = [sem(f"x_loaded{k}") for k in range(3)]
        y_ready = sem("y_ready")
        x_turned = sem("x_turned")
        rms_ready = sem("rms_ready")
        hi_ready = sem("hi_ready")
        lo_ready = sem("lo_ready")
        raw_loaded = [sem("raw_loaded0"), sem("raw_loaded1")]
        w_hi_ready = sem("w_hi_ready")
        w_lo_ready = sem("w_lo_ready")
        fa_loaded = sem("fa_loaded")
        fa_split = sem("fa_split")
        gate_w_loaded = sem("gate_w_loaded")
        gate_w_zero = sem("gate_w_zero")
        out_done = sem("out_done")
        out_used = sem("out_used")
        conv_ready = sem("conv_ready")
        root_ready = sem("root_ready")
        lru_done = sem("lru_done")
        lam_exp = sem("lam_exp")
        lam_ready = sem("lam_ready")
        stage_stored = [sem("stage_stored0"), sem("stage_stored1")]
        att_tables = sem("att_tables")
        fa_used = sem("fa_used")
        fa_turned = sem("fa_turned")
        fa_arg_ready = sem("fa_arg_ready")
        fa_exp_ready = sem("fa_exp_ready")
        fa_ready = sem("fa_ready")
        eps_ready = sem("eps_ready")
        lam_exp_ready = sem("lam_exp_ready")
        y_stored = sem("y_stored")
        logf_ready = sem("logf_ready")
        logf_turned = sem("logf_turned")
        cum_ready = sem("cum_ready")
        cum_stored = sem("cum_stored")
        cum_loaded = sem("cum_loaded")
        bf_loaded = sem("bf_loaded")
        clogf_loaded = sem("clogf_loaded")
        rel_loaded = sem("rel_loaded")
        rel_filled = sem("rel_filled")
        rel_stored = sem("rel_stored")
        rel_skewed = sem("rel_skewed")
        k_loaded = sem("k_loaded")
        v_loaded = sem("v_loaded")
        cache_loaded = sem("cache_loaded")
        turned = sem("turned")
        turned_used = sem("turned_used")
        state_turned = sem("state_turned")
        state_used = sem("state_used")
        rows_ready = sem("rows_ready")
        q_blocks_ready = sem("q_blocks_ready")
        scores_ready = sem("scores_ready")
        scores_used = sem("scores_used")
        exp_ready = sem("exp_ready")
        probs_ready = sem("probs_ready")
        probs_turned = sem("probs_turned")
        probs_t_ready = sem("probs_t_ready")
        att_out = sem("att_out")
        att_out_used = sem("att_out_used")
        res_loaded = sem("res_loaded")
        mixed = sem("mixed")
        mix_sq = sem("mix_sq")
        x1_ready = sem("x1_ready")
        x1_sq = sem("x1_sq")
        y2_ready = sem("y2_ready")
        y2_turned = sem("y2_turned")
        x1_stored = sem("x1_stored")
        h2_hi = sem("h2_hi")
        h2_lo = sem("h2_lo")
        low_banks_free = sem("low_banks_free")
        high_banks_free = sem("high_banks_free")
        group_added = sem("group_added")
        gate_done = sem("gate_done")
        val_done = sem("val_done")
        gate_evac = sem("gate_evac")
        fconv_ready = sem("fconv_ready")
        gelu_ready = sem("gelu_ready")
        f_ready = sem("f_ready")
        f_hi_ready = sem("f_hi_ready")
        f_lo_ready = sem("f_lo_ready")
        down_done = sem("down_done")
        added = sem("added")
        x1_loaded = sem("x1_loaded")
        f_sq = sem("f_sq")
        y_final = sem("y_final")
        ffn_turned = sem("ffn_turned")
        ffn_rows_ready = sem("ffn_rows_ready")
        stored = sem("stored")

        R_OUT = 2 * NU
        R_FFN = R_OUT + 8
        N_TURN_K = 6
        SEGMENTS = [("pf", 2 * N_TURN_K), ("sf", NS), ("pb", 0), ("sb", NS)]
        seg_steps = [[n for n, s_ in enumerate(STEPS) if s_[0] == kind] for kind, _ in SEGMENTS]

        block = ctx.enter_context(nc.Block())

        @block.sync
        def _(sp):
            for t in range(3):
                sp.dma_start(x_in[:, t, :], rows_of(xp, xs, t)).then_inc(x_loaded[t], 16)
            sp.dma_start(gains[:, 0, :], i["norm_g"][0, 0:1, :].to_broadcast([P, D])).then_inc(gain_loaded, 16)

            def load_half(r, dst, src):
                if r >= 2:
                    sp.wait_ge(w_lo_ready, r - 1)
                sp.dma_start(dst, src).then_inc(raw_loaded[r % 2], 16)

            def load_in(r):
                c0 = UNITS[r // 2][1]
                k0 = 4 * (r % 2)
                load_half(r, raw[:, r % 2, :].rearrange("p (k c) -> p k c", k=4),
                          w_in[k0 * P:(k0 + 4) * P, c0:c0 + 256].rearrange("(k p) c -> p k c", p=P))

            load_in(0)
            load_in(1)
            for t in range(3, NT):
                sp.wait_ge(y_ready, t - 2)
                sp.dma_start(x_in[:, t % 3, :], rows_of(xp, xs, t)).then_inc(x_loaded[t % 3], 16)
            for r in range(2, 2 * NU):
                load_in(r)
                if r == 4:
                    sp.dma_start(fa_raw[:, :, :], w_in[:, C_FA:C_FA + H].rearrange("(k p) c -> p k c", p=P))\
                      .then_inc(fa_loaded, 16)
            for q in range(8):
                r = R_OUT + q
                h, k0 = q // 4, 2 * (q % 4)
                load_half(r, raw[:, r % 2, :].rearrange("p (k c) -> p k c", k=2),
                          w_out[k0 * P:(k0 + 2) * P, h * 512:(h + 1) * 512].rearrange("(k p) c -> p k c", p=P))
            sp.wait_ge(y_ready, NT)
            for g in range(2):
                sp.dma_start(gains[:, g, :], i["norm_g"][0, 1 + g:2 + g, :].to_broadcast([P, D]))\
                  .then_inc(gain2_loaded, 16)
            for t in range(NT):
                if t == 0:
                    sp.wait_ge(att_out_used, NSTEP)
                else:
                    sp.wait_ge(x1_ready, t)
                sp.dma_start(x_res[:, :], rows_of(xp, xs, t)).then_inc(res_loaded, 16)

            def load_group(g, r0):
                for c in range(FG):
                    for half in range(2):
                        r = 2 * c + half
                        sp.wait_ge(w_lo_ready, r0 + r - 1)
                        sp.dma_start(raw[:, r % 2, :].rearrange("p (k c) -> p k c", k=KD),
                                     w_up[:, bass.ds(g * (FG * P) + (half * DFF + c * P), P)]
                                     .rearrange("(k p) c -> p k c", p=P)).then_inc(raw_loaded[r % 2], 16)
                for k in range(FG):
                    sp.wait_ge(w_lo_ready, r0 + 4 + k - 1)
                    sp.dma_start(raw[:, k, :], w_down[bass.ds(g * (FG * P) + k * P, P), :])\
                      .then_inc(raw_loaded[k], 16)

            with sp.Fori(0, NG) as g:
                load_group(g, g * 6 + R_FFN)
            sp.wait_ge(y2_ready, NT)
            sp.dma_start(gains[:, 0, :], i["norm_g"][0, 3:4, :].to_broadcast([P, D])).then_inc(gain3_loaded, 16)
            sp.wait_ge(x1_stored, 16 * NT)
            sp.wait_ge(val_done, FT)
            sp.dma_start(x1_back[:, :, :], x1_dram.rearrange("(c p) d -> p c d", p=P)).then_inc(x1_loaded, 16)
            for t in range(NT):
                sp.wait_ge(y_final, t + 1)
                sp.dma_start(rows_of(yp, ys, t), f_acc[:, t, :]).then_inc(y_stored, 16)
            sp.wait_ge(y_stored, 16 * NT)

        @block.gpsimd
        def _(pool):
            step = Chain(pool, pool_step)
            step(pool.memset(ident[:, :], 0.0))
            step(pool.affine_select(out=ident[:, :], in_=ident[:, :], compare_op=ALU.not_equal, fill=1.0, base=0,
                                    pattern=[[-1, P]], channel_multiplier=1))
            pool.tensor_copy(ident_b[:, :], ident[:, :]).then_inc(consts_ready, 1)
            step(pool.memset(cmask_b[:, :], 0.0))
            pool.affine_select(out=cmask_b[:, :], in_=cmask_b[:, :], compare_op=ALU.is_ge, fill=BIG, base=0,
                               pattern=[[-1, P]], channel_multiplier=1).then_inc(consts_ready, 1)
            step(pool.memset(chan_rows[:, :, :], 0.0))
            loads = [(0, 0, i["lru_conv_w"].rearrange("l k (j p) -> (l k j) p", p=P)),
                     (0, 16, i["lru_conv_b"].rearrange("l (j p) -> (l j) p", p=P)),
                     (0, 20, i["lru_ba"].rearrange("l (j p) -> (l j) p", p=P)),
                     (0, 24, i["lru_bx"].rearrange("l (j p) -> (l j) p", p=P)),
                     (0, 28, i["lru_lambda"].rearrange("l (j p) -> (l j) p", p=P)),
                     (0, 32, i["state_lru_h"].rearrange("l b (j p) -> (l b j) p", p=P)),
                     (1, 0, i["ffn_conv_w"].rearrange("l k (j p) -> (l k j) p", p=P)),
                     (1, 72, i["ffn_conv_b"].rearrange("l (j p) -> (l j) p", p=P)),
                     (2, 0, i["state_lru_conv"].rearrange("l b k (j p) -> (l b k j) p", p=P))]
            hist = i["state_ffn_conv"].rearrange("l b k (j p) -> (l b k j) p", p=P)
            loads += [(3 + c, 0, hist[c * P:(c + 1) * P, :]) for c in range(3)]
            for slot, row, src in loads:
                pool.dma_start(chan_rows[row:row + src.shape[0], slot, :], src).then_inc(chan_loaded, 16)
            assert len(loads) == 12
            step(pool.memset(gate_w[:, :, :, :], 0.0))
            for k, name in enumerate(("lru_wa", "lru_wx")):
                src = i[name][0].rearrange("(j two) d e -> two d j e", two=2)
                for two in range(2):
                    pool.dma_start(gate_w[64 * two:64 * two + 64, k, :, 64 * two:64 * two + 64], src[two])\
                        .then_inc(gate_w_loaded, 16)
            for s, lot in enumerate(STORES):
                pool.wait_ge(out_used, KV_OUTS[s] + 1)
                for name, t0, n, c in lot:
                    dst = kv_dram.get(name)
                    if dst is None:
                        dst = kv_out[name]
                    row0 = t0 - (4 if name in ("bk_p", "bv_p") else 0)
                    row0 = 0 if name.endswith("_s") else row0
                    pool.dma_start(tile_rows(dst, row0, n), stage[:, s % 2, c:c + n, :])\
                        .then_inc(stage_stored[s % 2], 16)

            last = len(STORES) - 1
            for q in range(2):
                pool.wait_ge(stage_stored[q], 16 * stores_until(q, last))
            pool.wait_ge(out_done, NO)
            pool.wait_ge(lru_done, LT)
            pool.wait_ge(out_used, NO - 1)
            pool.dma_start(k_rows[:, 0:NPT, :], tile_rows(kv_out["fk_p"], 0, NPT)).then_inc(k_loaded, 16)
            pool.dma_start(k_rows[:, NPT:NT, :], tile_rows(kv_out["fk_s"], 0, 1)).then_inc(k_loaded, 16)
            pool.dma_start(v_f[:, 0:NPT, :], tile_rows(kv_out["fv_p"], 0, NPT)).then_inc(v_loaded, 16)
            pool.dma_start(v_f[:, NPT:NT, :], tile_rows(kv_out["fv_s"], 0, 1)).then_inc(v_loaded, 16)
            bf = stat[:, BF_:BF_ + H]
            pool.dma_start(bf, i["b_forget"].to_broadcast([P, H])).then_inc(bf_loaded, 16)
            step(pool.memset(upper[:, :], 1.0))
            pool.affine_select(out=upper[:, :], in_=upper[:, :], compare_op=ALU.is_ge, fill=0.0, base=0,
                               pattern=[[1, SK]], channel_multiplier=-1).then_inc(att_tables, 1)
            blk = stat[:, BLK:BLK + NS]
            step(pool.memset(blk, 1.0))
            step(pool.affine_select(out=blk, in_=blk, compare_op=ALU.is_ge, fill=0.0, base=0,
                                    pattern=[[-TS, NS]], channel_multiplier=1))
            pool.affine_select(out=blk, in_=blk, compare_op=ALU.is_ge, fill=0.0, base=TS - 1,
                               pattern=[[TS, NS]], channel_multiplier=-1).then_inc(att_tables, 1)
            future = logf_new[:, 0:2, :].rearrange("p a c -> p (a c)").rearrange("p (g c) -> p g c", g=NS)
            step(pool.memset(future, BIG))
            pool.affine_select(out=future, in_=future, compare_op=ALU.is_gt, fill=0.0, base=0,
                               pattern=[[TS, NS], [1, TS]], channel_multiplier=-1).then_inc(att_tables, 1)
            pool.dma_start(cache_logf[:, :, :].rearrange("p (b k) h -> p b k h", k=2),
                           i["cache_fox_logf"][0].rearrange("b (k p) h -> p b k h", p=P)).then_inc(clogf_loaded, 16)

            def load_caches(k_name, v_name):
                for dst, name in ((cache_k, k_name), (cache_v, v_name)):
                    src = i[name][0].rearrange("b (k p) h d -> p b k (h d)", p=P)
                    for half in range(2):
                        pool.dma_start(dst[:, 4 * half:4 * half + 4, :, :], src[:, 4 * half:4 * half + 4])\
                            .then_inc(cache_loaded, 16)

            load_caches("cache_fox_k", "cache_fox_v")
            pool.wait_ge(logf_ready, 1)
            pool.dma_start(o["fox_logf_p"].rearrange("l b (c p) h -> p (l b c) h", p=P), logf[:, 0:NPT, :])\
                .then_inc(stored, 16)
            pool.dma_start(o["fox_logf_s"].rearrange("l b s h -> (l b s) h"), logf[:, NPT, :]).then_inc(stored, 16)
            pool.wait_ge(cum_ready, 1)
            pool.dma_start(cum_dram, cum_rows).then_inc(cum_stored, 16)
            pool.wait_ge(cum_stored, 16)
            pool.dma_start(cum_b[:, :, :], cum_dram.rearrange("(a h) c -> a h c", a=1).to_broadcast([P, H, SEQ]))\
                .then_inc(cum_loaded, 16)
            pool.wait_ge(turned_used, N_TURN_K)
            pool.dma_start(rel_rows[:, :, 127:127 + NREL],
                           i["rel_bias"][0:1, :, :].to_broadcast([P, H, NREL])).then_inc(rel_loaded, 16)
            pool.wait_ge(rel_filled, 1)
            pool.dma_start(rel_dram.ap(), k_rows[:, 0:6, :].rearrange("p a b -> p (a b)")).then_inc(rel_stored, 16)
            pool.wait_ge(rel_stored, 16)
            pitch = H * 384
            skewed = bass.AP(rel_dram, 127, [[pitch - 1, P], [384, H], [1, 256]])
            pool.dma_start(band_bias[:, :, BANDW - 256:], skewed).then_inc(rel_skewed, 16)
            for b2 in range(2):
                for h in range(H):
                    src = bass.AP(rel_dram, 127 + h * 384, [[pitch - 1, TS], [1, P + TS]])
                    row = 64 * b2 + TS * h
                    pool.dma_start(band_bias_s[row:row + TS, P:SK], src).then_inc(rel_skewed, 16)
            pool.dma_start(k_rows[:, :, :], tile_rows(kv_dram["bk_scr"], 0, NT)).then_inc(k_loaded, 16)
            pool.dma_start(v_b[:, :, :], tile_rows(kv_dram["bv_scr"], 0, NT)).then_inc(v_loaded, 16)
            pool.wait_ge(rows_ready, 1)
            for name, r0, n in (("lru_h_p", 0, 1), ("lru_h_s", 1, NS)):
                pool.dma_start(o[name].rearrange("l b c -> (l b) c"), state_rows[r0:r0 + n, :]).then_inc(stored, 16)
            for name, r0, n in (("lru_conv_p", 9, LH), ("lru_conv_s", 12, NS * LH)):
                pool.dma_start(o[name].rearrange("l b k c -> (l b k) c"), state_rows[r0:r0 + n, :]).then_inc(stored, 16)
            pool.wait_ge(att_out, seg_steps[1][-1] + 1)
            load_caches("cache_band_k", "cache_band_v")

            for t in range(NT):
                pool.wait_ge(x1_ready, t + 1)
                pool.dma_start(x1_dram[t * P:(t + 1) * P, :], x1[:, :]).then_inc(x1_stored, 16)
            pool.wait_ge(ffn_rows_ready, 6)
            pool.dma_start(o["ffn_conv_p"].rearrange("l b k c -> (l b k) c"), ffn_rows[0:FH, :]).then_inc(stored, 16)
            pool.dma_start(o["ffn_conv_s"].rearrange("l b k c -> (l b k) c"), ffn_rows[FH:18, :]).then_inc(stored, 16)
            pool.wait_ge(stored, 16 * 8)

        @block.scalar
        def _(act):
            step = Chain(act, act_step)

            def norm_hi(t):
                act.wait_ge(x_turned, t + 1)
                act.activation(act_hi[:, :, t * P:(t + 1) * P],
                               PS[:, 2 * (t % 2):2 * (t % 2) + 2, :].rearrange("p b (k c) -> p (b k) c", c=P),
                               ACT.Copy).then_inc(hi_ready, 1)

            act.wait_ge(chan_turned, 1)
            act.activation(chan[:, 0:4, :].rearrange("p s c -> p (s c)"), PS[:, 6, :], ACT.Copy).then_inc(chan_ready, 1)
            act.activation(chan[:, 4:6, :].rearrange("p s c -> p (s c)"), PS[:, 7, 0:256], ACT.Copy)\
               .then_inc(chan_ready, 1)
            for t in range(NT):
                act.wait_ge(x_loaded[t % 3], 16 * (t // 3 + 1))
                step(act.activation(square0[:, :], x_in[:, t % 3, :], ACT.Square,
                                    accum_out=stat[:, SS0 + t:SS0 + t + 1]))
                if t == 0:
                    act.wait_ge(eps_ready, 1)
                act.activation(stat[:, RM0 + t:RM0 + t + 1], stat[:, SS0 + t:SS0 + t + 1], ACT.Sqrt,
                               scale=1.0 / D, bias=stat[:, EPSC:EPSC + 1]).then_inc(rms_ready, 1)
                if t >= 1:
                    norm_hi(t - 1)
            norm_hi(NT - 1)
            act.wait_ge(lam_exp, 1)
            act.activation(stat[:, TMP + LT:TMP + 2 * LT], stat[:, TMP:TMP + LT], ACT.Exp, scale=-1.0)\
               .then_inc(lam_exp_ready, 1)

            def split_hi(r, dst):
                act.wait_ge(raw_loaded[r % 2], 16 * (r // 2 + 1))
                act.activation(dst, raw[:, r % 2, :], ACT.Copy).then_inc(w_hi_ready, 1)

            def split_unit(u):
                if u >= 3:
                    act.wait_ge(out_done, last_output(u - 3) + 1)
                for half in range(2):
                    split_hi(2 * u + half, w_hi[:, u % 3, half * 1024:(half + 1) * 1024])

            for u in range(3):
                split_unit(u)
            act.wait_ge(fa_loaded, 16)
            act.activation(fa_hi[:, :, :], fa_raw[:, :, :], ACT.Copy).then_inc(fa_split, 1)
            staged = 0
            for n, (kind, u, j) in enumerate(OUTS):
                banks = PS[:, 3 * (n % 2):3 * (n % 2) + 3, :]
                if kind == "x":
                    act.wait_ge(out_done, n + 1)
                    act.activation(mix[:, MIX_OF_X[j], :].rearrange("p (b c) -> p b c", b=3), banks[:, :, 0:CW],
                                   ACT.Copy).then_inc(out_used, 1)
                elif kind == "y":
                    act.wait_ge(out_done, n + 1)
                    act.activation(mix[:, 2 + j, :].rearrange("p (b c) -> p b c", b=3), banks[:, :, 0:CW],
                                   ACT.Gelu_apprx_tanh).then_inc(out_used, 1)
                elif kind in ("gate_r", "gate_i"):
                    if kind == "gate_r" and j >= 1:
                        act.wait_ge(lru_done, j)
                    act.wait_ge(out_done, n + 1)
                    g = 0 if kind == "gate_r" else 1
                    act.activation((gate_r, gate_i)[g][:, :].rearrange("p (b c) -> p b c", b=3),
                                   banks[:, :, 0:LW // 3], ACT.Sigmoid, bias=lru_const(5 + g, j)).then_inc(out_used, 1)
                    if g:
                        act.wait_ge(out_used, n + 1)
                        if j == 0:
                            act.wait_ge(lam_ready, 1)
                        step(act.activation(gate_r[:, :], gate_r[:, :], ACT.Tanh, scale=stat[:, SP4 + j:SP4 + j + 1]))
                        act.activation(xpad[:, 0:LW], gate_r[:, :], ACT.Sqrt).then_inc(root_ready, 1)
                elif kind in KV:
                    if staged >= 2:
                        act.wait_ge(stage_stored[staged % 2], 16 * stores_until(staged % 2, staged - 2))
                    act.wait_ge(out_done, n + 1)
                    act.activation(stage[:, staged % 2, :, :], banks[:, :, 0:DH], ACT.Copy).then_inc(out_used, 1)
                    staged += 1
                elif kind in ("fq", "bq"):
                    act.wait_ge(conv_ready, LT)
                    act.wait_ge(out_done, n + 1)
                    act.activation(mix[:, (0 if kind == "fq" else 6) + j, :].rearrange("p (b c) -> p b c", b=3),
                                   banks[:, :, 0:CW], ACT.Copy, scale=QS).then_inc(out_used, 1)
                elif kind == "fa":
                    act.wait_ge(lru_done, LT)
                    for q in range(2):
                        act.wait_ge(stage_stored[q], 16 * stores_until(q, len(STORES) - 1))
                    act.wait_ge(out_done, n + 1)
                    act.activation(fa_rows.rearrange("p (b c) -> p b c", b=3), banks[0:H, :, 0:CW], ACT.Copy)\
                       .then_inc(out_used, 1)
                if u is not None and n == last_output(u) and u + 3 < NU:
                    split_unit(u + 3)

            act.wait_ge(fa_arg_ready, 1)
            act.activation(stat[:, TMP + 72:TMP + 108], stat[:, TMP + 36:TMP + 72], ACT.Exp, scale=-1.0)\
               .then_inc(fa_exp_ready, 1)
            act.wait_ge(state_turned, 1)
            act.activation(state_rows[0:36, :], PS[0:36, 7, :], ACT.Copy).then_inc(rows_ready, 1)

            def used_batch(q, dst, width):
                act.wait_ge(turned, q + 1)
                act.activation(dst, PS[:, q % 4, 0:width], ACT.Copy).then_inc(turned_used, 1)

            def key_batches(q0, kt):
                for q in range(N_TURN_K):
                    ct, part = q // 3, q % 3
                    n = 4 if part < 2 else 1
                    used_batch(q0 + q, kt[:, ct, part * 512:part * 512 + n * P], n * P)

            def cache_batches(q0):
                for b in range(NS):
                    used_batch(q0 + b, kt_s[:, b, :, :].rearrange("p t c -> p (t c)"), 512)

            def widths(n):
                st = STEPS[n]
                return SK if st[0][0] == "s" else P * key_blocks(st)[1]

            def turned_back(n):
                act.wait_ge(probs_turned, n + 1)
                if n >= 2:
                    act.wait_ge(att_out, n - 1)
                if n == 1:
                    act.wait_ge(stored, 16 * 6)
                w = 3 * P if STEPS[n][0][0] == "s" else widths(n)
                act.activation(probs_t[:, n % 2, 0:w], PS[:, 4:6, :].rearrange("p b c -> p (b c)")[:, 0:w], ACT.Copy)\
                   .then_inc(probs_t_ready, 1)

            q0 = 0
            for (kind, batches), steps in zip(SEGMENTS, seg_steps):
                if kind == "pf":
                    key_batches(0, kt_f)
                    key_batches(N_TURN_K, kt_b)
                elif batches:
                    cache_batches(q0)
                q0 += batches
                for n in steps:
                    act.wait_ge(scores_used, n + 1)
                    act.activation(probs[:, n % 2, 0:widths(n)], probs[:, n % 2, 0:widths(n)], ACT.Exp, scale=-1.0,
                                   bias=stat[:, RMIN + n % 2:RMIN + n % 2 + 1],
                                   accum_out=stat[:, RSUM + n % 2:RSUM + n % 2 + 1]).then_inc(exp_ready, 1)
                    if n > steps[0]:
                        turned_back(n - 1)
                turned_back(steps[-1])

            for q in range(8):
                dst = w_hi[:, q // 2, (q % 2) * 1024:(q % 2 + 1) * 1024] if q < 6 else \
                    wx_hi[:, (q - 6) * 1024:(q - 5) * 1024]
                if q == 0:
                    act.wait_ge(att_out_used, NSTEP)
                split_hi(R_OUT + q, dst)
            for t in range(NT):
                act.activation(act_hi[:, :, t * P:(t + 1) * P], mix[:, :, t * P:(t + 1) * P], ACT.Copy)\
                   .then_inc(hi_ready, 1)

            def h2_half(t):
                act.wait_ge(y2_turned, t + 1)
                act.activation(act_hi[:, :, t * P:(t + 1) * P],
                               PS[:, 4:6, :].rearrange("p b (k c) -> p (b k) c", c=P), ACT.Copy).then_inc(h2_hi, 1)

            for t in range(NT):
                s0 = 2 * (t % 2)
                act.wait_ge(mixed, t + 1)
                step(act.activation(PS[:, 6:8, :], PS[:, s0:s0 + 2, :], ACT.Square,
                                    accum_out=stat[:, SS1 + t:SS1 + t + 1]))
                act.activation(stat[:, SS1 + t:SS1 + t + 1], stat[:, SS1 + t:SS1 + t + 1], ACT.Sqrt, scale=1.0 / D,
                               bias=stat[:, EPSC:EPSC + 1]).then_inc(mix_sq, 1)
                act.wait_ge(x1_ready, t + 1)
                step(act.activation(PS[:, 6:8, :].rearrange("p b c -> p (b c)"), x1[:, :], ACT.Square,
                                    accum_out=stat[:, SS2 + t:SS2 + t + 1]))
                act.activation(stat[:, SS2 + t:SS2 + t + 1], stat[:, SS2 + t:SS2 + t + 1], ACT.Sqrt, scale=1.0 / D,
                               bias=stat[:, EPSC:EPSC + 1]).then_inc(x1_sq, 1)
                h2_half(t)

            def split_group_half(q, r0, k):
                act.wait_ge(raw_loaded[k % 2], q)
                act.activation(w_hi[:, k // 2, (k % 2) * 1024:(k % 2 + 1) * 1024], raw[:, k % 2, :], ACT.Copy)\
                   .then_inc(w_hi_ready, 1)

            def landed(g, k):
                return (g * 3 + (R_FFN // 2 + k // 2 + 1)) * 16

            act.wait_ge(mixed, NT)
            for k in range(6):
                split_group_half(landed(0, k), R_FFN, k)

            def ffn_tile(j, c):
                if c:
                    act.wait_ge(f_lo_ready, j)
                act.wait_ge(gate_done, j + 1)
                act.activation(gate_pad[:, FH:FH + 2 * CW].rearrange("p (b c) -> p b c", b=2), PS[:, 0:2, 0:CW],
                               ACT.Copy)
                act.activation(gate_pad[:, FH + 2 * CW:FH + SEQ], PS[:, 2, 0:SEQ - 2 * CW], ACT.Copy)
                act.activation(gate_pad[:, FH + SEQ:].rearrange("p (b c) -> p b c", b=NS)[:, :, FH:],
                               PS[:, 2, SEQ - 2 * CW:CW].rearrange("p (b c) -> p b c", b=NS), ACT.Copy)\
                   .then_inc(gate_evac, 1)
                act.wait_ge(fconv_ready, j + 1)
                act.activation(gate_conv[:, :], gate_conv[:, :], ACT.Gelu_apprx_tanh).then_inc(gelu_ready, 1)

            def ffn_hi(j, c):
                act.wait_ge(f_ready, j + 1)
                act.activation(f_hi[:, c, :], gate_pad[:, FH:FH + T], ACT.Copy).then_inc(f_hi_ready, 1)

            def ffn_group(g, more):
                for c in range(FG):
                    ffn_tile(g * FG + c, c)
                    ffn_hi(g * FG + c, c)
                    if more:
                        act.wait_ge(val_done, g * FG + (c + 1))
                        for half in range(2):
                            split_group_half(landed(g + 1, 2 * c + half), None, 2 * c + half)
                if more:
                    act.wait_ge(down_done, g * 18 + 18)
                    for k in range(4, 6):
                        split_group_half(landed(g + 1, k), None, k)

            with act.Fori(0, NG - 1) as g:
                ffn_group(g, True)
            ffn_group(NG - 1, False)
            for t in range(NT):
                act.wait_ge(added, 18 * NG + 2 * t + 2)
                step(act.activation(square3[:, :], f_acc[:, t, :], ACT.Square,
                                    accum_out=stat[:, SS3 + t:SS3 + t + 1]))
                act.activation(stat[:, SS3 + t:SS3 + t + 1], stat[:, SS3 + t:SS3 + t + 1], ACT.Sqrt, scale=1.0 / D,
                               bias=stat[:, EPSC:EPSC + 1]).then_inc(f_sq, 1)
            for q in range(6):
                act.wait_ge(ffn_turned, q + 1)
                act.activation(ffn_rows[:, q * 512:(q + 1) * 512], PS[0:18, q, :], ACT.Copy).then_inc(ffn_rows_ready, 1)

        @block.vector
        def _(dve):
            step = Chain(dve, dve_step)

            def subtract(out, a, hi):
                return dve.tensor_tensor(out, a, hi.bitcast(F32), ALU.subtract)

            def softplus_of_minus(out, z, e, n, tmp):
                q, q2, s = (stat[:, tmp + k * n:tmp + (k + 1) * n] for k in range(3))
                step(dve.tensor_scalar(q, e, 2.0, None, ALU.add))
                step(dve.reciprocal(q, q))
                step(dve.tensor_tensor(q, q, e, ALU.mult))
                step(dve.tensor_tensor(q2, q, q, ALU.mult))
                step(dve.tensor_scalar(s, q2, 1.0 / 17, None, ALU.mult))
                for k in (15, 13, 11, 9, 7, 5, 3):
                    step(dve.scalar_tensor_tensor(s, s, 1.0 / k, q2, ALU.add, ALU.mult))
                step(dve.scalar_tensor_tensor(s, s, 1.0, q, ALU.add, ALU.mult))
                step(dve.tensor_scalar(q, z, -1.0, 0.0, ALU.mult, ALU.max))
                return dve.scalar_tensor_tensor(out, s, 2.0, q, ALU.mult, ALU.add)

            def norm_lo(t):
                dve.wait_ge(hi_ready, t + 1)
                cols = slice(t * P, (t + 1) * P)
                subtract(act_lo[:, :, cols], PS[:, 2 * (t % 2):2 * (t % 2) + 2, :].rearrange("p b (k c) -> p (b k) c", c=P),
                         act_hi[:, :, cols]).then_inc(lo_ready, 1)

            dve.memset(stat[:, EPSC:EPSC + 1], EPS).then_inc(eps_ready, 1)
            dve.wait_ge(gain_loaded, 16)
            for t in range(NT):
                dve.wait_ge(rms_ready, t + 1)
                step(dve.reciprocal(stat[:, RR0 + t:RR0 + t + 1], stat[:, RM0 + t:RM0 + t + 1]))
                if t >= 2:
                    dve.wait_ge(x_turned, t - 1)
                dve.scalar_tensor_tensor(y_in[:, t % 2, :], x_in[:, t % 3, :], stat[:, RR0 + t:RR0 + t + 1],
                                         gains[:, 0, :], ALU.mult, ALU.mult).then_inc(y_ready, 1)
                if t >= 1:
                    norm_lo(t - 1)
            norm_lo(NT - 1)
            dve.wait_ge(chan_ready, 2)
            dve.scalar_tensor_tensor(stat[:, TMP:TMP + LT], lam, -1.0, lam, ALU.mult, ALU.max).then_inc(lam_exp, 1)
            dve.wait_ge(lam_exp_ready, 1)
            step(softplus_of_minus(stat[:, SP4:SP4 + LT], lam, stat[:, TMP + LT:TMP + 2 * LT], LT, TMP + 2 * LT))
            dve.tensor_scalar(stat[:, SP4:SP4 + LT], stat[:, SP4:SP4 + LT], 4.0, None, ALU.mult).then_inc(lam_ready, 1)

            def split_lo(r, hi, lo):
                dve.wait_ge(w_hi_ready, r + 1)
                subtract(lo, raw[:, r % 2, :], hi).then_inc(w_lo_ready, 1)

            def split_unit(u):
                for half in range(2):
                    cols = slice(half * 1024, (half + 1) * 1024)
                    split_lo(2 * u + half, w_hi[:, u % 3, cols], w_lo[:, u % 3, cols])

            pitch = LH + TS

            def lru_conv(j):
                x = mix[:, MIX_OF_X[j], :]
                dve.wait_ge(out_used, OUTS.index(("x", j // 2, j)) + 1)
                dve.memset(xpad[:, 0:LH], 0.0)
                dve.tensor_copy(xpad[:, LH:LH + SEQ], x[:, 0:SEQ])
                pads = xpad[:, LH + SEQ:LPAD].rearrange("p (b c) -> p b c", b=NS)
                news = x[:, SEQ:T].rearrange("p (b c) -> p b c", b=NS)
                dve.tensor_copy(pads[:, :, LH:], news)
                dve.tensor_copy(pads[:, :, 0:LH], lru_hist[:, :, :, j])
                dve.tensor_copy(lru_state[:, j, 9:9 + LH], x[:, SEQ - LH:SEQ])
                step(dve.tensor_copy(lru_state[:, j, 12:36].rearrange("p (b k) -> p b k", b=NS), news[:, :, TS - LH:]))
                step(dve.tensor_scalar(xconv[:, :], xpad[:, 0:LW], lru_const(0, j), lru_const(4, j), ALU.mult, ALU.add))
                for k in range(1, LCONV):
                    ins = dve.scalar_tensor_tensor(xconv[:, :], xpad[:, k:k + LW], lru_const(k, j), xconv[:, :],
                                                   ALU.mult, ALU.add)
                    if k < LCONV - 1:
                        step(ins)
                ins.then_inc(conv_ready, 1)

            def lru_scan(j):
                dve.wait_ge(root_ready, j + 1)
                step(dve.tensor_tensor(gate_i[:, :], gate_i[:, :], xconv[:, :], ALU.mult))
                step(dve.tensor_scalar(gate_r[:, :], gate_r[:, :], 1.0, None, ALU.add))
                step(dve.reciprocal(gate_r[:, :], gate_r[:, :]))
                dve.tensor_scalar(xconv[:, :], gate_r[:, :], 2.0, -1.0, ALU.mult, ALU.add)
                step(dve.tensor_tensor(xpad[:, 0:LW], xpad[:, 0:LW], gate_r[:, :], ALU.mult))
                step(dve.scalar_tensor_tensor(gate_i[:, :], gate_i[:, :], 2.0, xpad[:, 0:LW], ALU.mult, ALU.mult))
                starts = slice(SEQ + LH - 1, SEQ + LH - 1 + pitch * (NS - 1) + 1, pitch)
                dve.memset(xconv[:, starts], 0.0)
                step(dve.tensor_copy(gate_i[:, starts], h0[:, :, j]))
                step(dve.tensor_tensor_scan(gate_r[:, :], xconv[:, :], gate_i[:, :], 0.0, ALU.mult, ALU.add))
                first = SEQ + LH
                y = mix[:, 2 + j, :]
                dve.wait_ge(out_used, OUTS.index(("y", 2 + j // 2, j)) + 1)
                dve.tensor_tensor(y[:, 0:SEQ], y[:, 0:SEQ], gate_r[:, 0:SEQ], ALU.mult)
                ys_ = y[:, SEQ:T].rearrange("p (b c) -> p b c", b=NS)
                last = first + (NS - 1) * pitch
                dve.tensor_tensor(ys_[:, 0:NS - 1, :], ys_[:, 0:NS - 1, :],
                                  gate_r[:, first:last].rearrange("p (b c) -> p b c", c=pitch)[:, :, 0:TS], ALU.mult)
                dve.tensor_tensor(ys_[:, NS - 1, :], ys_[:, NS - 1, :], gate_r[:, last:last + TS], ALU.mult)
                dve.tensor_copy(lru_state[:, j, 0:1], gate_r[:, SEQ - 1:SEQ])
                dve.tensor_copy(lru_state[:, j, 1:9], gate_r[:, first + TS - 1:last + TS:pitch]).then_inc(lru_done, 1)

            for u in range(3):
                split_unit(u)
            dve.wait_ge(fa_split, 1)
            subtract(fa_lo[:, :, :], fa_raw[:, :, :], fa_hi[:, :, :]).then_inc(fa_ready, 1)
            lru_conv(0)
            split_unit(3)
            split_unit(4)
            for j in range(LT):
                lru_scan(j)
                if j < LT - 1:
                    split_unit(5 + j)
                    lru_conv(j + 1)
            for u in range(8, NU):
                split_unit(u)

            z, az, e = (stat[:, TMP + 36 * k:TMP + 36 * (k + 1)] for k in range(3))
            dve.wait_ge(bf_loaded, 16)
            dve.wait_ge(fa_turned, 1)
            bf = stat[:, BF_:BF_ + H].rearrange("p (a h) -> p a h", a=1).to_broadcast([P, NT, H])
            step(dve.tensor_tensor(z.rearrange("p (t h) -> p t h", h=H),
                                   PS[:, 6, 0:NT * H].rearrange("p (t h) -> p t h", h=H), bf, ALU.add))
            dve.scalar_tensor_tensor(az, z, -1.0, z, ALU.mult, ALU.max).then_inc(fa_arg_ready, 1)
            dve.wait_ge(fa_exp_ready, 1)
            step(softplus_of_minus(az, z, e, 36, TMP + 36 * 3))
            dve.tensor_scalar(logf[:, :, :].rearrange("p t h -> p (t h)"), az, -1.0, None, ALU.mult)\
               .then_inc(logf_ready, 1)
            step(dve.memset(one_rows, 1.0))
            dve.wait_ge(logf_turned, 1)
            dve.tensor_tensor_scan(cum_rows, one_rows, PS[0:H, 4:6, :].rearrange("p b c -> p (b c)"), 0.0,
                                   ALU.mult, ALU.add).then_inc(cum_ready, 1)

            dve.wait_ge(logf_ready, 1)
            dve.wait_ge(att_tables, 3)
            blk = stat[:, BLK:BLK + NS]
            future = logf_new[:, 0:2, :].rearrange("p a c -> p (a c)").rearrange("p (g c) -> p g c", g=NS)
            step(dve.memset(fox_mask_s[:, 0:PAST], 0.0))
            step(dve.tensor_tensor(future, future, blk.rearrange("p (g a) -> p g a", a=1).to_broadcast([P, NS, TS]),
                                   ALU.mult))
            step(dve.tensor_reduce(fox_mask_s[:, PAST:SK], future.rearrange("p g c -> p c g"), AX.X, ALU.add))
            new = logf[:, NPT, :].rearrange("p (h a) -> p h a", a=1).to_broadcast([P, H, TS])
            for b in range(NS):
                dve.tensor_scalar(logf_new[:, b, :].rearrange("p (h c) -> p h c", h=H), new, blk[:, b:b + 1], None,
                                  ALU.mult)
            dve.wait_ge(clogf_loaded, 16)
            dve.tensor_copy(logf_rows[:, :, :].rearrange("p k (h c) -> p (k h) c", h=H),
                            cache_logf[:, :, :].rearrange("p k (h a) -> p (k h) a", a=1)
                            .to_broadcast([P, 2 * NS * H, TS]))
            step(dve.memset(q_blocks[:, :, :, :], 0.0))

            def spread_queries(tile0):
                for h in range(H):
                    t, rows = h // 2, slice(64 * (h % 2), 64 * (h % 2) + 64)
                    last = dve.tensor_copy(q_blocks[rows, :, t, TS * h:TS * (h + 1)],
                                           mix[rows, tile0 + t, SEQ:T].rearrange("p (b c) -> p b c", b=NS))
                last.then_inc(q_blocks_ready, 1)

            dve.wait_ge(out_used, NO)
            spread_queries(0)

            dve.wait_ge(rel_loaded, 16)
            dve.memset(rel_rows[:, :, 127 + NREL:384], 0.0)
            dve.tensor_copy(rel_rows[:, :, 0:127], rel_rows[:, :, 127:128].to_broadcast([P, H, 127]))\
               .then_inc(rel_filled, 1)

            def band_tables():
                dve.wait_ge(rel_skewed, 16 * (1 + 2 * H))
                step(dve.tensor_scalar(band_bias[:, :, BANDW - 256:], band_bias[:, :, BANDW - 256:], -1.0, None,
                                       ALU.mult))
                step(dve.tensor_copy(band_bias[:, :, 0:BANDW - 256],
                                     band_bias[:, :, BANDW - 256:BANDW - 255].to_broadcast([P, H, BANDW - 256])))
                dve.memset(band_bias[0:64, :, BANDW - CHUNK:], BIG)
                dve.memset(band_bias[64:P, :, 0:CHUNK], BIG)
                step(dve.tensor_scalar(band_bias_s[:, P:SK], band_bias_s[:, P:SK], -1.0, None, ALU.mult))
                step(dve.tensor_copy(band_bias_s[:, 0:P], band_bias_s[:, P:P + 1].to_broadcast([P, P])))

            def take_scores(n):
                st, s = STEPS[n], n % 2
                if st[0] == "sf":
                    w, bias = SK, fox_mask_s[:, :]
                elif st[0] == "sb":
                    w, bias = SK, band_bias_s[:, :]
                elif st[0] == "pf":
                    w = P * key_blocks(st)[1]
                    bias = cum_b[:, st[1], 0:w]
                else:
                    w = P * key_blocks(st)[1]
                    bias = band_bias[:, st[1], BANDW - w:BANDW]
                dve.wait_ge(scores_ready, n + 1)
                if n >= 2:
                    dve.wait_ge(probs_turned, n - 1)
                src = PS[:, 2 * s:2 * s + 2, :].rearrange("p b c -> p (b c)")[:, 0:w]
                dve.tensor_tensor_reduce(out=probs[:, s, 0:w], in0=src, in1=bias, scale=1.0, scalar=START,
                                         op0=ALU.add, op1=ALU.min, accum_out=stat[:, RMIN + s:RMIN + s + 1])\
                   .then_inc(scores_used, 1)

            def normalise(n):
                st, s = STEPS[n], n % 2
                inv = stat[:, RINV + s:RINV + s + 1]
                if st[0][0] == "s":
                    step(dve.memset(probs[:, s, 512:512 + P], 0.0))
                dve.wait_ge(exp_ready, n + 1)
                step(dve.reciprocal(inv, stat[:, RSUM + s:RSUM + s + 1]))
                if st[0][0] == "s":
                    for b2 in range(2):
                        rows, c0 = slice(64 * b2, 64 * b2 + 64), 512 + TS * (2 * st[1] + b2)
                        dve.tensor_scalar(probs[rows, s, c0:c0 + TS], probs[rows, s, PAST:SK],
                                          stat[rows, RINV + s:RINV + s + 1], None, ALU.mult)
                    w = PAST
                else:
                    w = P * key_blocks(st)[1]
                dve.tensor_scalar(probs[:, s, 0:w], probs[:, s, 0:w], inv, None, ALU.mult).then_inc(probs_ready, 1)

            def take_output(n):
                st, bank = STEPS[n], 6 + n % 2
                dve.wait_ge(att_out, n + 1)
                if st[0][0] == "s":
                    tile0 = 0 if st[0] == "sf" else 6
                    for h in range(H):
                        t, rows = h // 2, slice(64 * (h % 2), 64 * (h % 2) + 64)
                        c0 = SEQ + 2 * TS * st[1]
                        last = dve.tensor_copy(
                            mix[rows, tile0 + t, c0:c0 + 2 * TS].rearrange("p (b c) -> p b c", b=2),
                            PS[rows, bank, 128 * t:128 * t + 128].rearrange("p (b c) -> p b c", b=2)
                            [:, :, TS * h:TS * (h + 1)])
                    last.then_inc(att_out_used, 1)
                else:
                    h, q = st[1], st[2]
                    rows = slice(64 * (h % 2), 64 * (h % 2) + 64)
                    dve.tensor_copy(mix[rows, (0 if st[0] == "pf" else 6) + h // 2, q * P:(q + 1) * P],
                                    PS[rows, bank, 0:P]).then_inc(att_out_used, 1)

            for (kind, _), steps in zip(SEGMENTS, seg_steps):
                if kind == "pf":
                    dve.wait_ge(cum_loaded, 16)
                if kind == "sf":
                    band_tables()
                if kind == "sb":
                    spread_queries(6)
                for n in steps:
                    take_scores(n)
                    if n - 2 >= steps[0]:
                        take_output(n - 2)
                    normalise(n)
                take_output(steps[-1] - 1)
                take_output(steps[-1])

            for q in range(8):
                k, half = q // 2, slice((q % 2) * 1024, (q % 2 + 1) * 1024)
                hi, lo = (w_hi[:, k, half], w_lo[:, k, half]) if q < 6 else (wx_hi[:, half], wx_lo[:, half])
                split_lo(R_OUT + q, hi, lo)
            for t in range(NT):
                cols = slice(t * P, (t + 1) * P)
                dve.wait_ge(hi_ready, NT + t + 1)
                subtract(act_lo[:, :, cols], mix[:, :, cols], act_hi[:, :, cols]).then_inc(lo_ready, 1)
            dve.wait_ge(gain2_loaded, 32)
            for t in range(NT):
                s0 = 2 * (t % 2)
                cols = slice(t * P, (t + 1) * P)
                dve.wait_ge(mix_sq, t + 1)
                inv = stat[:, SS1 + t:SS1 + t + 1]
                step(dve.reciprocal(inv, inv))
                if t >= 1:
                    dve.wait_ge(x1_stored, 16 * t)
                step(dve.scalar_tensor_tensor(x1[:, :], PS[:, s0:s0 + 2, :].rearrange("p b c -> p (b c)"), inv,
                                              gains[:, 0, :], ALU.mult, ALU.mult))
                dve.wait_ge(res_loaded, 16 * (t + 1))
                dve.tensor_tensor(x1[:, :], x1[:, :], x_res[:, :], ALU.add).then_inc(x1_ready, 1)
                dve.wait_ge(x1_sq, t + 1)
                inv = stat[:, SS2 + t:SS2 + t + 1]
                step(dve.reciprocal(inv, inv))
                dve.scalar_tensor_tensor(y2[:, :], x1[:, :], inv, gains[:, 1, :], ALU.mult, ALU.mult)\
                   .then_inc(y2_ready, 1)
                dve.wait_ge(h2_hi, t + 1)
                subtract(act_lo[:, :, cols], PS[:, 4:6, :].rearrange("p b (k c) -> p (b k) c", c=P), act_hi[:, :, cols])\
                    .then_inc(h2_lo, 1)

            dve.wait_ge(x1_stored, 16 * NT)
            dve.wait_ge(mixed, NT)
            for t in range(NT):
                for half in range(2):
                    dve.memset(f_acc[:, t, half * 512:(half + 1) * 512], 0.0).then_inc(added, 1)
            step(dve.memset(gate_pad[:, 0:FH], 0.0))

            def split_group_half(r, k):
                cols = slice((k % 2) * 1024, (k % 2 + 1) * 1024)
                dve.wait_ge(w_hi_ready, r + 1)
                subtract(w_lo[:, k // 2, cols], raw[:, k % 2, :], w_hi[:, k // 2, cols]).then_inc(w_lo_ready, 1)

            for k in range(6):
                split_group_half(R_FFN + k, k)
            fpitch = FH + TS
            pads = gate_pad[:, FH + SEQ:FPAD].rearrange("p (b c) -> p b c", b=NS)

            def ffn_tile(j, c):
                if c:
                    dve.wait_ge(f_lo_ready, j)
                dve.tensor_copy(pads[:, :, 0:FH], ffn_hist[:, :, :, bass.ds(j, 1)].rearrange("p b k a -> p b (k a)"))
                dve.wait_ge(gate_evac, j + 1)
                state = ffn_state[:, bass.ds(j, 1), :].rearrange("p a c -> p (a c)")
                dve.tensor_copy(state[:, 0:FH], gate_pad[:, SEQ:SEQ + FH])
                step(dve.tensor_copy(state[:, FH:].rearrange("p (b k) -> p b k", b=NS), pads[:, :, TS:]))
                step(dve.tensor_scalar(gate_conv[:, :], gate_pad[:, 0:FW], ffn_const[:, bass.ds(j, 1)],
                                       ffn_const[:, bass.ds(j + FCONV * FT, 1)], ALU.mult, ALU.add))
                step(dve.scalar_tensor_tensor(gate_conv[:, :], gate_pad[:, 1:1 + FW], ffn_const[:, bass.ds(j + FT, 1)],
                                              gate_conv[:, :], ALU.mult, ALU.add))
                dve.scalar_tensor_tensor(gate_conv[:, :], gate_pad[:, 2:2 + FW], ffn_const[:, bass.ds(j + 2 * FT, 1)],
                                         gate_conv[:, :], ALU.mult, ALU.add).then_inc(fconv_ready, 1)
                dve.wait_ge(val_done, j + 1)
                dve.wait_ge(gelu_ready, j + 1)
                dve.tensor_tensor(gate_pad[:, FH:FH + 2 * CW].rearrange("p (b c) -> p b c", b=2), PS[:, 3:5, 0:CW],
                                  gate_conv[:, 0:2 * CW].rearrange("p (b c) -> p b c", b=2), ALU.mult)
                dve.tensor_tensor(gate_pad[:, FH + 2 * CW:FH + SEQ], PS[:, 5, 0:SEQ - 2 * CW],
                                  gate_conv[:, 2 * CW:SEQ], ALU.mult)
                first = SEQ + FH
                dve.tensor_tensor(gate_pad[:, FH + SEQ:FH + T - TS].rearrange("p (b c) -> p b c", c=TS),
                                  PS[:, 5, SEQ - 2 * CW:CW - TS].rearrange("p (b c) -> p b c", c=TS),
                                  gate_conv[:, first:first + (NS - 1) * fpitch]
                                  .rearrange("p (b c) -> p b c", c=fpitch)[:, :, 0:TS], ALU.mult)
                dve.tensor_tensor(gate_pad[:, FH + T - TS:FH + T], PS[:, 5, CW - TS:CW],
                                  gate_conv[:, FW - TS:FW], ALU.mult).then_inc(f_ready, 1)
                dve.wait_ge(f_hi_ready, j + 1)
                subtract(f_lo[:, c, :], gate_pad[:, FH:FH + T], f_hi[:, c, :]).then_inc(f_lo_ready, 1)

            def add_output(g, q):
                dve.wait_ge(down_done, g * 18 + (q + 1))
                acc = f_acc[:, q // 2, (q % 2) * 512:(q % 2 + 1) * 512]
                dve.tensor_tensor(acc, acc, PS[:, bank_of(q), :], ALU.add).then_inc(added, 1)

            def ffn_tiles(g, more):
                for c in range(FG):
                    ffn_tile(g * FG + c, c)
                    if more:
                        for half in range(2):
                            split_group_half(g * 6 + (R_FFN + 6 + 2 * c + half), 2 * c + half)

            before = step.n
            steps_of_group = 3 * FG
            with dve.Fori(0, NG - 1) as g:
                step.base, step.n = g * steps_of_group + before, 0
                ffn_tiles(g, True)
                assert step.n == steps_of_group
                for q in range(18):
                    add_output(g, q)
                for k in range(4, 6):
                    split_group_half(g * 6 + (R_FFN + 6 + k), k)
            step.base, step.n = 0, before + (NG - 1) * steps_of_group
            ffn_tiles(NG - 1, False)

            def finish(t):
                dve.wait_ge(f_sq, t + 1)
                inv = stat[:, SS3 + t:SS3 + t + 1]
                step(dve.reciprocal(inv, inv))
                step(dve.scalar_tensor_tensor(f_acc[:, t, :], f_acc[:, t, :], inv, gains[:, 0, :],
                                              ALU.mult, ALU.mult))
                dve.tensor_tensor(f_acc[:, t, :], f_acc[:, t, :], x1_back[:, t, :], ALU.add).then_inc(y_final, 1)

            dve.wait_ge(gain3_loaded, 16)
            for t in range(NT):
                add_output(NG - 1, 2 * t)
                add_output(NG - 1, 2 * t + 1)
                if t == 1:
                    dve.wait_ge(x1_loaded, 16)
                if t >= 1:
                    finish(t - 1)
            finish(NT - 1)

        @block.tensor
        def _(pe):
            bank_cols = lambda b, w: PS[:, b, 0:w]

            def turn(out, in_, rows=P):
                return pe.transpose(out, in_, ident[0:rows, 0:rows])

            pe.wait_ge(consts_ready, 2)
            pe.wait_ge(chan_loaded, 16 * 12)
            for s in range(6):
                last = turn(PS[:, 6 + s // 4, (s % 4) * P:(s % 4 + 1) * P], chan_rows[:, s, :])
            last.then_inc(chan_turned, 1)
            for t in range(NT):
                pe.wait_ge(y_ready, t + 1)
                if t >= 2:
                    pe.wait_ge(lo_ready, t - 1)
                for k in range(KD):
                    last = turn(PS[:, 2 * (t % 2) + k // 4, (k % 4) * P:(k % 4 + 1) * P],
                                y_in[:, t % 2, k * P:(k + 1) * P])
                last.then_inc(x_turned, 1)

            acts = (act_hi, act_lo)

            def channels_out(banks, w, width=P):
                for n, (wp, ap) in enumerate(((0, 0), (0, 1), (1, 0))):
                    for k in range(KD):
                        for c in range(3):
                            last = pe.matmul(PS[0:width, banks + c, 0:CW], w(wp, k),
                                             acts[ap][:, k, c * CW:(c + 1) * CW],
                                             start=(n == 0 and k == 0), stop=(n == 2 and k == KD - 1))
                return last

            pe.wait_ge(lo_ready, NT)
            seen = set()
            for n, (kind, u, j) in enumerate(OUTS):
                b0 = 3 * (n % 2)
                if n >= 2:
                    pe.wait_ge(out_used, n - 1)
                if u is not None and u not in seen:
                    seen.add(u)
                    pe.wait_ge(w_lo_ready, 2 * u + 2)
                    w_units = [w[:, u % 3, :].rearrange("p (k c) -> p k c", k=KD) for w in (w_hi, w_lo)]
                if kind in ("x", "y", "fq", "bq"):
                    last = channels_out(b0, lambda part, k: w_units[part][:, k, (j % 2) * P:(j % 2 + 1) * P])
                elif kind in KV:
                    for m, (ap, wp) in enumerate(((0, 0), (0, 1), (1, 0))):
                        for k in range(KD):
                            for c in range(3):
                                t = 3 * j + c
                                last = pe.matmul(bank_cols(b0 + c, DH), acts[ap][:, k, t * P:(t + 1) * P],
                                                 w_units[wp][:, k, :], start=(m == 0 and k == 0),
                                                 stop=(m == 2 and k == KD - 1))
                elif kind in ("gate_r", "gate_i"):
                    pe.wait_ge(conv_ready, j + 1)
                    pe.wait_ge(gate_w_loaded, 64)
                    for c in range(3):
                        last = pe.matmul(bank_cols(b0 + c, LW // 3), gate_w[:, int(kind == "gate_i"), j, :],
                                         xconv[:, c * (LW // 3):(c + 1) * (LW // 3)], start=True, stop=True)
                else:
                    pe.wait_ge(fa_ready, 1)
                    last = channels_out(b0, lambda part, k: (fa_hi, fa_lo)[part][:, k, :], H)
                last.then_inc(out_done, 1)

            pe.wait_ge(out_used, NO)
            for t in range(NT):
                last = turn(PS[:, 6, t * H:(t + 1) * H], fa_rows[:, t * P:(t + 1) * P], H)
            last.then_inc(fa_turned, 1)
            for j in range(LT):
                last = turn(PS[0:36, 7, j * P:(j + 1) * P], lru_state[:, j, :])
            last.then_inc(state_turned, 1)

            def key_batches(q0, need):
                pe.wait_ge(k_loaded, need)
                for q in range(q0, q0 + N_TURN_K):
                    ct, part = (q - q0) // 3, (q - q0) % 3
                    if q >= 4:
                        pe.wait_ge(turned_used, q - 3)
                    for c in range(4 if part < 2 else 1):
                        last = turn(PS[:, q % 4, c * P:(c + 1) * P], k_rows[:, 4 * part + c, ct * P:(ct + 1) * P])
                    last.then_inc(turned, 1)

            def cache_batches(q0, need):
                pe.wait_ge(cache_loaded, need)
                for b in range(NS):
                    q = q0 + b
                    pe.wait_ge(turned_used, q - 3)
                    for t in range(2):
                        for k in range(2):
                            c = 2 * t + k
                            last = turn(PS[:, q % 4, c * P:(c + 1) * P], cache_k[:, b, k, t * P:(t + 1) * P])
                    last.then_inc(turned, 1)

            def scores(n):
                st, s = STEPS[n], n % 2
                if n >= 2:
                    pe.wait_ge(scores_used, n - 1)
                if st[0][0] == "p":
                    h, q = st[1], st[2]
                    rows, t = slice(64 * (h % 2), 64 * (h % 2) + 64), h // 2
                    kt, tile = (kt_f, t) if st[0] == "pf" else (kt_b, 6 + t)
                    k0, nk = key_blocks(st)
                    for b in range((nk + 3) // 4):
                        n_b = min(4, nk - 4 * b)
                        c0 = (k0 + 4 * b) * P
                        diag = st[0] == "pf" and b == (nk - 1) // 4
                        last = pe.matmul(PS[:, 2 * s + b, 0:n_b * P], mix[rows, tile, q * P:(q + 1) * P],
                                         kt[rows, t, c0:c0 + n_b * P], start=True, stop=not diag)
                        if diag:
                            last = pe.matmul(PS[:, 2 * s + b, (n_b - 1) * P:n_b * P], ident_b[:, :], cmask_b[:, :],
                                             start=False, stop=True)
                else:
                    kt = kt_f if st[0] == "sf" else kt_b
                    for b2 in range(2):
                        b = 2 * st[1] + b2
                        out = PS[64 * b2:64 * b2 + 64, 2 * s, :]
                        fox = st[0] == "sf"
                        for t in range(2):
                            last = pe.matmul(out[:, 0:PAST], q_blocks[:, b, t, :], kt_s[:, b, t, :],
                                             start=t == 0, stop=(t == 1 and not fox))
                        if fox:
                            pe.matmul(out[:, 0:PAST], logf_rows[:, 2 * b, :], upper[:, 0:PAST], start=False, stop=False)
                            last = pe.matmul(out[:, P:PAST], logf_rows[:, 2 * b + 1, :], upper[:, 0:P],
                                             start=False, stop=True)
                        c0 = SEQ + TS * b
                        for t in range(2):
                            last = pe.matmul(out[:, PAST:SK], q_blocks[:, b, t, :], kt[:, t, c0:c0 + TS],
                                             start=t == 0, stop=(t == 1 and not fox))
                        if fox:
                            pe.matmul(out[:, PAST:SK], logf_rows[:, 2 * b, :], upper[:, PAST:SK], start=False, stop=False)
                            pe.matmul(out[:, PAST:SK], logf_rows[:, 2 * b + 1, :], upper[:, P:P + TS],
                                      start=False, stop=False)
                            last = pe.matmul(out[:, PAST:SK], logf_new[:, b, :], upper[:, TS * b:TS * (b + 1)],
                                             start=False, stop=True)
                last.then_inc(scores_ready, 1)

            def turn_probs(n):
                st, s = STEPS[n], n % 2
                pe.wait_ge(probs_ready, n + 1)
                if n >= 1:
                    pe.wait_ge(probs_t_ready, n)
                blocks = (0, P, 512) if st[0][0] == "s" else [P * b for b in range(key_blocks(st)[1])]
                for b, c0 in enumerate(blocks):
                    last = turn(PS[:, 4 + b // 4, (b % 4) * P:(b % 4 + 1) * P], probs[:, s, c0:c0 + P])
                last.then_inc(probs_turned, 1)

            def values(n):
                st, s = STEPS[n], n % 2
                pe.wait_ge(probs_t_ready, n + 1)
                if n >= 2:
                    pe.wait_ge(att_out_used, n - 1)
                if st[0][0] == "p":
                    h = st[1]
                    v = v_f if st[0] == "pf" else v_b
                    k0, nk = key_blocks(st)
                    for b in range(nk):
                        last = pe.matmul(PS[64 * (h % 2):64 * (h % 2) + 64, 6 + s, 0:P],
                                         v[:, k0 + b, HD * h:HD * (h + 1)], probs_t[:, s, b * P:(b + 1) * P],
                                         start=b == 0, stop=b == nk - 1)
                else:
                    v = v_f if st[0] == "sf" else v_b
                    for t in range(2):
                        for b2 in range(2):
                            b = 2 * st[1] + b2
                            out = PS[:, 6 + s, (2 * t + b2) * 64:(2 * t + b2 + 1) * 64]
                            for k in range(3):
                                vals = cache_v[:, b, k, t * P:(t + 1) * P] if k < 2 else v[:, NPT, t * P:(t + 1) * P]
                                last = pe.matmul(out, vals, probs_t[:, s, k * P + 64 * b2:k * P + 64 * b2 + 64],
                                                 start=k == 0, stop=k == 2)
                last.then_inc(att_out, 1)

            key_batches(0, 32)
            pe.wait_ge(logf_ready, 1)
            for t in range(NPT):
                last = turn(PS[0:H, 4 + t // 4, (t % 4) * P:(t % 4 + 1) * P], logf[:, t, :])
            last.then_inc(logf_turned, 1)
            key_batches(N_TURN_K, 48)
            q0 = 2 * N_TURN_K
            for (kind, batches), steps in zip(SEGMENTS, seg_steps):
                if kind == "pf":
                    pe.wait_ge(cum_ready, 1)
                    pe.wait_ge(v_loaded, 32)
                    pe.wait_ge(rows_ready, 1)
                elif batches:
                    pe.wait_ge(scores_used, steps[0])
                    cache_batches(q0, 64 if kind == "sf" else 128)
                    q0 += batches
                    pe.wait_ge(q_blocks_ready, 1 if kind == "sf" else 2)
                else:
                    pe.wait_ge(v_loaded, 48)
                pe.wait_ge(turned_used, q0)
                scores(steps[0])
                for n in steps:
                    if n < steps[-1]:
                        scores(n + 1)
                    if n > steps[0]:
                        values(n - 1)
                    turn_probs(n)
                values(steps[-1])

            def turn_y2(t):
                pe.wait_ge(y2_ready, t + 1)
                if t >= 1:
                    pe.wait_ge(h2_lo, t)
                for k in range(KD):
                    last = turn(PS[:, 4 + k // 4, (k % 4) * P:(k % 4 + 1) * P], y2[:, k * P:(k + 1) * P])
                last.then_inc(y2_turned, 1)

            def wout_tile(part, h, k):
                q = 2 * h + k // 4
                w = (w_hi, w_lo)[part][:, q, :] if q < 3 else (wx_hi, wx_lo)[part][:, :]
                return w[:, (k % 4) * 512:(k % 4 + 1) * 512]

            pe.wait_ge(att_out_used, NSTEP)
            pe.wait_ge(w_lo_ready, R_OUT + 8)
            for t in range(NT):
                pe.wait_ge(lo_ready, NT + t + 1)
                if t >= 2:
                    pe.wait_ge(x1_ready, t - 1)
                for h in range(2):
                    for m, (ap, wp) in enumerate(((0, 0), (0, 1), (1, 0))):
                        for k in range(KD):
                            last = pe.matmul(PS[:, 2 * (t % 2) + h, :], acts[ap][:, k, t * P:(t + 1) * P],
                                             wout_tile(wp, h, k), start=(m == 0 and k == 0),
                                             stop=(m == 2 and k == KD - 1))
                last.then_inc(mixed, 1)
                if t >= 1:
                    turn_y2(t - 1)
            turn_y2(NT - 1)

            pe.wait_ge(h2_lo, NT)

            def down(g, q, ks):
                t, cols = q // 2, slice((q % 2) * 512, (q % 2 + 1) * 512)
                for k in ks:
                    for m, (fp, wp) in enumerate(((0, 0), (0, 1), (1, 0))):
                        w = (w_hi, w_lo)[wp][:, 2, :].rearrange("p (k c) -> p k c", k=FG)[:, k, cols]
                        last = pe.matmul(PS[:, bank_of(q), :], (f_hi, f_lo)[fp][:, k, t * P:(t + 1) * P], w,
                                         start=(k == 0 and m == 0), stop=(k == FG - 1 and m == 2))
                if ks[-1] == FG - 1:
                    last.then_inc(down_done, 1)

            def ffn_group(g):
                for c in range(FG):
                    j = g * FG + c
                    for half in range(2):
                        pe.wait_ge(w_lo_ready, g * 6 + (R_FFN + 2 * c + half + 1))
                        if c == 0:
                            pe.wait_ge(added, g * 18 + (13, 16)[half])
                        else:
                            pe.wait_ge((gate_evac, f_ready)[half], j)
                        w = [x[:, c, half * 1024:(half + 1) * 1024].rearrange("p (k c) -> p k c", k=KD)
                             for x in (w_hi, w_lo)]
                        channels_out(3 * half, lambda part, k: w[part][:, k, :])\
                            .then_inc((gate_done, val_done)[half], 1)
                pe.wait_ge(w_lo_ready, g * 6 + (R_FFN + 6))
                pe.wait_ge(f_lo_ready, g * FG + 1)
                pe.wait_ge(added, g * 18 + 18)
                for q in range(8):
                    if q == 2:
                        pe.wait_ge(gate_evac, g * FG + FG)
                    if q == 5:
                        pe.wait_ge(f_ready, g * FG + FG)
                    down(g, q, [0])
                pe.wait_ge(f_lo_ready, g * FG + FG)
                for q in range(8):
                    down(g, q, [1])
                for q in range(8, 18):
                    pe.wait_ge(added, g * 18 + (18 + q - 7))
                    down(g, q, [0, 1])

            with pe.Fori(0, NG) as g:
                ffn_group(g)

            pe.wait_ge(added, 18 * NG + 18)
            for q in range(6):
                for c in range(4):
                    last = turn(PS[0:18, q, c * P:(c + 1) * P], ffn_state[:, 4 * q + c, :])
                last.then_inc(ffn_turned, 1)


_NAMES = ["x_prompt", "x_sample", "cache_fox_k", "cache_fox_v", "cache_fox_logf", "cache_band_k", "cache_band_v",
          "state_lru_h", "state_lru_conv", "state_ffn_conv", "norm_g", "w_in", "b_forget", "lru_conv_w", "lru_conv_b",
          "lru_wa", "lru_ba", "lru_wx", "lru_bx", "lru_lambda", "rel_bias", "w_out", "w_up", "ffn_conv_w",
          "ffn_conv_b", "w_down"]
_KEEP = CHUNK * 8
_OUTPUTS = [("y_prompt", (1, SEQ, D)), ("y_sample", (NS, TS, D)),
            ("fox_k_p", (1, 1, SEQ, H, HD)), ("fox_k_s", (1, NS, TS, H, HD)),
            ("fox_v_p", (1, 1, SEQ, H, HD)), ("fox_v_s", (1, NS, TS, H, HD)),
            ("fox_logf_p", (1, 1, SEQ, H)), ("fox_logf_s", (1, NS, TS, H)),
            ("band_k_p", (1, 1, _KEEP, H, HD)), ("band_k_s", (1, NS, TS, H, HD)),
            ("band_v_p", (1, 1, _KEEP, H, HD)), ("band_v_s", (1, NS, TS, H, HD)),
            ("lru_h_p", (1, 1, DL)), ("lru_h_s", (1, NS, DL)),
            ("lru_conv_p", (1, 1, LH, DL)), ("lru_conv_s", (1, NS, LH, DL)),
            ("ffn_conv_p", (1, 1, FH, DFF)), ("ffn_conv_s", (1, NS, FH, DFF))]


def kernel(**inputs):
    import numpy as np
    import concourse.bacc as bacc
    from concourse.bass_utils import run_bass_kernel_spmd

    nc = bacc.Bacc("TRN2", target_bir_lowering=False, num_devices=1)
    arrays, ins, outs = {}, {}, {}
    for name in _NAMES:
        a = np.ascontiguousarray(inputs[name])
        arrays[f"in_{name}"] = a
        ins[name] = nc.dram_tensor(f"in_{name}", a.shape, mybir.dt.from_np(a.dtype), kind="ExternalInput").ap()
    for name, shape in _OUTPUTS:
        outs[name] = nc.dram_tensor(f"out_{name}", shape, F32, kind="ExternalOutput").ap()
    encoder_step(nc, ins, outs)
    r = run_bass_kernel_spmd(nc, [arrays], core_ids=[0])
    return tuple(r.results[0][f"out_{name}"] for name, _ in _OUTPUTS)
```

```python
from contextlib import ExitStack

import concourse.bass as bass
from concourse import mybir

F32 = mybir.dt.float32
F32R = mybir.dt.float32r
BF16 = mybir.dt.bfloat16
ALU = mybir.AluOpType
ACT = mybir.ActivationFunctionType
AX = mybir.AxisListType

P = 128
D = 1024
KD = D // P
SEQ = 1024
NPT = SEQ // P
NS, TS = 8, 16
T = SEQ + NS * TS
NT = T // P
CW = T // 3
PAST = 256
CHUNK, HD = 64, 64
H = 4
DH = H * HD
DL = 512
LT = DL // P
LCONV, FCONV = 4, 3
DFF = 3072
FT = DFF // P
FG = 2
NG = FT // FG
NREL = 192
BANDW = 640
EPS = 1e-6
QS = -(HD ** -0.5)
BIG = 1e30
START = 3e38
SK = PAST + TS

LH = LCONV - 1
LPAD = LH + SEQ + NS * (LH + TS)
LW = LPAD - LH
FH = FCONV - 1
FPAD = FH + SEQ + NS * (FH + TS)
FW = FPAD - FH

C_FQ, C_FK, C_FV, C_FA = 0, DH, 2 * DH, 3 * DH
C_X = 3 * DH + H
C_Y = C_X + DL
C_BQ = C_Y + DL
C_BK, C_BV = C_BQ + DH, C_BQ + 2 * DH

UNITS = [("x", C_X), ("x", C_X + 256), ("y", C_Y), ("y", C_Y + 256), ("fk", C_FK), ("fv", C_FV),
         ("bk", C_BK), ("bv", C_BV), ("fq", C_FQ), ("bq", C_BQ)]
KV = ("fk", "fv", "bk", "bv")
NU = len(UNITS)
MIX_OF_X = [0, 1, 6, 7]


def projection_outputs():
    outs = []
    for u, (kind, _) in enumerate(UNITS):
        first = {"x": 2 * u, "y": 2 * (u - 2)}.get(kind, 0)
        outs += [(kind, u, first + c) for c in range(3 if kind in KV else 2)]
    for j, after in enumerate(GATES_AFTER):
        at = outs.index(after) + 1
        outs[at:at] = [("gate_r", None, j), ("gate_i", None, j)]
    at = outs.index(("bv", 7, 2)) + 1
    outs[at:at] = [("fa", None, 0)]
    return outs


GATES_AFTER = [("y", 2, 0), ("y", 3, 3), ("fk", 4, 2), ("fv", 5, 2)]
OUTS = projection_outputs()
NO = len(OUTS)


KV_OUTS = [n for n, out in enumerate(OUTS) if out[0] in KV]


def last_output(u):
    return max(n for n, o in enumerate(OUTS) if o[1] == u)


def attention_steps():
    fox = [("pf", h, i) for i in range(NPT) for h in range(H)]
    band = [("pb", h, i) for i in range(NPT) for h in range(H)]
    pairs = range(NS // 2)

    def with_turns(turns, steps):
        mixed = [x for p, turn in enumerate(turns) for x in (turn, steps[2 * p], steps[2 * p + 1])]
        return mixed + steps[2 * len(turns):]

    cached = [("kt", p) for p in pairs]
    fox_turns, band_turns = ([(k, c) for c in range(3)] for k in ("kf", "kb"))
    return (fox_turns + fox[:18] + with_turns(band_turns + cached, fox[18:]) + [("sf", p) for p in pairs] + band[:7] + with_turns(cached, band[7:16]) + [("sb", p) for p in pairs]
            + band[16:])


STEPS = attention_steps()
NSTEP = len(STEPS)
REAL = [n for n, st in enumerate(STEPS) if st[0][0] != "k"]
COUNT = {n: r for r, n in enumerate(REAL)}
NREAL = len(REAL)
KEY_TURNS = [n for n, st in enumerate(STEPS) if st[0] == "kt"]
FIRST = {kind: min(n for n in REAL if STEPS[n][0] == kind) for kind in ("pf", "sf", "pb", "sb")}
LAST = {kind: max(n for n in REAL if STEPS[n][0] == kind) for kind in ("pf", "sf", "pb", "sb")}
REL_FILL_AT, SAMPLE_TABLES_AT, BAND_TABLES_AT = 9, (13, 15, 17), FIRST["sf"] - 12
OUT_SPLITS = [LAST["sb"] + 3 + 2 * q for q in range(6)]


def key_blocks(step):
    if step[0] == "pf":
        return 0, step[2] + 1
    first = max(0, step[2] - 4)
    return first, step[2] - first + 1


def stage_stores():
    lots = []
    for kind in KV:
        for tg in range(3):
            t0 = 3 * tg
            np_ = 3 if tg < 2 else 2
            if kind[0] == "f":
                lot = [(kind + "_p", t0, np_, 0)]
            else:
                lot = [(kind + "_scr", t0, 3, 0)]
                if tg == 1:
                    lot.append((kind + "_p", 4, 2, 1))
                if tg == 2:
                    lot.append((kind + "_p", 6, 2, 0))
            if tg == 2:
                lot.append((kind + "_s", 8, 1, 2))
            lots.append(lot)
    return lots


STORES = stage_stores()


def stores_until(slot, s):
    return sum(len(STORES[q]) for q in range(s + 1) if q % 2 == slot)


def bank_of(q):
    return (6 + q) % 8


class Chain:

    def __init__(self, eng, sem):
        self.eng, self.sem, self.base, self.n = eng, sem, 0, 0

    def __call__(self, ins):
        self.n += 1
        ins.then_inc(self.sem, 1)
        self.eng.wait_ge(self.sem, self.base + self.n)


def encoder_step(nc, i, o):
    with ExitStack() as ctx:
        def sb(name, shape, dt=F32, stack=ctx):
            return stack.enter_context(nc.sbuf_tensor(name, shape, dt))

        def sem(name):
            return ctx.enter_context(nc.semaphore(name))

        ident = sb("ident", [P, P])
        ident_b = sb("ident_b", [P, P], BF16)
        cmask_b = sb("cmask_b", [P, P], BF16)
        chan = sb("chan", [P, 6, P])
        gains = sb("gains", [P, 2, D])
        lru_state = sb("lru_state", [P, LT, 36])
        stat = sb("stat", [P, 320])
        logf = sb("logf", [P, NT, H])

        with ExitStack() as s:
            act_hi = sb("act_hi", [P, KD, T], F32R, s)
            act_lo = sb("act_lo", [P, KD, T], F32R, s)
        with ExitStack() as s:
            kt_f = sb("kt_f", [P, 2, T], F32, s)
            kt_b = sb("kt_b", [P, 2, T], F32, s)
            v_f = sb("v_f", [P, NT, DH], F32, s)
            v_b = sb("v_b", [P, NT, DH], F32, s)
            cache_v = sb("cache_v", [P, NS, 2, DH], F32, s)
            band_bias = sb("band_bias", [P, H, BANDW], F32, s)
            q_blocks = sb("q_blocks", [P, NS, 2, 64], F32, s)
            logf_rows = sb("logf_rows", [P, 2 * NS, 64], F32, s)
            logf_new = sb("logf_new", [P, NS, 64], F32, s)
        with ExitStack() as s:
            x1_back = sb("x1_back", [P, NT, D], F32, s)
            ffn_rows = sb("ffn_rows", [18, DFF], F32, s)
            square3 = sb("square3", [P, D], F32, s)
        sb("region_a", [P, 2 * KD * T])
        with ExitStack() as s:
            w_hi = sb("w_hi", [P, 3, 2048], F32R, s)
            w_lo = sb("w_lo", [P, 3, 2048], F32R, s)
        with ExitStack() as s:
            cache_k_low = sb("cache_k_low", [P, NS // 2, 2, DH], F32, s)
            cum_b = sb("cum_b", [P, H, SEQ], F32, s)
            kt_s = sb("kt_s", [P, NS, 2, PAST], F32, s)
            cache_k_high = sb("cache_k_high", [P, NS // 2, 2, DH], F32, s)
        sb("region_w", [P, 2 * 3 * 2048])
        raw = sb("raw", [P, 2, 1024])
        with ExitStack() as s:
            x_in = sb("x_in", [P, 3, D], F32, s)
            y_in = sb("y_in", [P, 2, D], F32, s)
            square0 = sb("square0", [P, D], F32, s)
            chan_rows = sb("chan_rows", [P, 6, P], F32, s)
        with ExitStack() as s:
            f_acc = sb("f_acc", [P, NT, D], F32, s)
            f_hi = sb("f_hi", [P, FG, T], F32R, s)
            f_lo = sb("f_lo", [P, FG, T], F32R, s)
            gate_pad = sb("gate_pad", [P, FPAD], F32, s)
            gate_conv = sb("gate_conv", [P, FW], F32, s)
            ffn_state = sb("ffn_state", [P, FT, 18], F32, s)
        mix = sb("mix", [P, KD, T])
        with ExitStack() as s:
            gate_w = sb("gate_w", [P, 2, LT, P], F32, s)
            xpad = sb("xpad", [P, LPAD], F32, s)
            xconv = sb("xconv", [P, LW], F32, s)
            gate_r = sb("gate_r", [P, LW], F32, s)
            gate_i = sb("gate_i", [P, LW], F32, s)
            stage = sb("stage", [P, 2, 3, DH], F32, s)
            fa_raw = sb("fa_raw", [P, KD, H], F32, s)
            fa_hi = sb("fa_hi", [P, KD, H], F32R, s)
            fa_lo = sb("fa_lo", [P, KD, H], F32R, s)
        with ExitStack() as s:
            probs = sb("probs", [P, 2, 1024], F32, s)
            probs_t = sb("probs_t", [P, 2, 1024], F32, s)
            k_rows = sb("k_rows", [P, NT, DH], F32, s)
            fox_mask_s = sb("fox_mask_s", [P, SK], F32, s)
            band_bias_s = sb("band_bias_s", [P, SK], F32, s)
            upper = sb("upper", [P, SK], F32, s)
            cache_logf = sb("cache_logf", [P, 2 * NS, H], F32, s)
        with ExitStack() as s:
            wx_hi = sb("wx_hi", [P, 2048], F32R, s)
            wx_lo = sb("wx_lo", [P, 2048], F32R, s)
            x_res = sb("x_res", [P, D], F32, s)
            x1 = sb("x1", [P, D], F32, s)
            y2 = sb("y2", [P, D], F32, s)
        fa_rows = probs_t[0:H, :, :].rearrange("p a b -> p (a b)")[:, 0:T]
        cum_rows = probs[0:H, 0, 0:SEQ]
        one_rows = probs[0:H, 1, 0:SEQ]
        rel_rows = k_rows[:, 0:6, :].rearrange("p a b -> p (a b)").rearrange("p (h c) -> p h c", h=H)
        state_rows = probs_t[:, 1, 512:1024]

        PS = ctx.enter_context(nc.psum_tensor("PS", [P, 8, 512], F32))

        x1_dram = nc.dram_tensor("x1_scratch", [T, D], F32, kind="Internal").ap()
        cum_dram = nc.dram_tensor("cum_scratch", [H, SEQ], F32, kind="Internal").ap()
        rel_dram = nc.dram_tensor("rel_scratch", [P, H * 384], F32, kind="Internal")
        kv_dram = {k + "_scr": nc.dram_tensor(k + "_scratch", [T, DH], F32, kind="Internal").ap() for k in ("bk", "bv")}
        kv_out = {}
        for kind, name in (("fk", "fox_k"), ("fv", "fox_v"), ("bk", "band_k"), ("bv", "band_v")):
            kv_out[kind + "_p"] = o[name + "_p"].rearrange("l b s h d -> (l b s) (h d)")
            kv_out[kind + "_s"] = o[name + "_s"].rearrange("l b s h d -> (l b s) (h d)")
        xp = i["x_prompt"].rearrange("b s d -> (b s) d")
        xs = i["x_sample"].rearrange("b s d -> (b s) d")
        yp = o["y_prompt"].rearrange("b s d -> (b s) d")
        ys = o["y_sample"].rearrange("b s d -> (b s) d")
        w_in = i["w_in"][0]
        w_out = i["w_out"][0]
        w_up = i["w_up"][0]
        w_down = i["w_down"][0]

        def rows_of(p_ap, s_ap, t):
            return p_ap[t * P:(t + 1) * P, :] if t < NPT else s_ap

        def tile_rows(ap, t0, n):
            return ap[t0 * P:(t0 + n) * P, :].rearrange("(c p) d -> p c d", p=P)

        def lru_const(k, j):
            return chan[:, 0, k * LT + j:k * LT + j + 1]
        lam = chan[:, 0, 7 * LT:8 * LT]
        h0 = chan[:, 0, 32:64].rearrange("p (b j) -> p b j", j=LT)
        lru_hist = chan[:, 2, 0:96].rearrange("p (b k j) -> p b k j", k=LH, j=LT)
        ffn_const = chan[:, 1, 0:96]
        ffn_hist = chan[:, 3:6, :].rearrange("p s c -> p (s c)").rearrange("p (b k j) -> p b k j", k=FH, j=FT)

        SS0, RM0, RR0 = 0, 9, 18
        SP4, SP8 = 28, 44
        EPSC = 32
        RMIN, RSUM, RINV = 34, 38, 42
        SS1, SS2, SS3 = 48, 57, 66
        BF_ = 76
        BLK = 80
        TMP = 88

        chan_loaded = sem("chan_loaded")
        chan_turned = sem("chan_turned")
        chan_ready = sem("chan_ready")
        gain_loaded = sem("gain_loaded")
        gain2_loaded = sem("gain2_loaded")
        gain3_loaded = sem("gain3_loaded")
        consts_ready = sem("consts_ready")
        pool_step = sem("pool_step")
        act_step = sem("act_step")
        dve_step = sem("dve_step")
        x_loaded = [sem(f"x_loaded{k}") for k in range(3)]
        y_ready = sem("y_ready")
        x_turned = sem("x_turned")
        rms_ready = sem("rms_ready")
        hi_ready = sem("hi_ready")
        lo_ready = sem("lo_ready")
        raw_loaded = [sem("raw_loaded0"), sem("raw_loaded1")]
        w_hi_ready = sem("w_hi_ready")
        w_lo_ready = sem("w_lo_ready")
        fa_loaded = sem("fa_loaded")
        fa_split = sem("fa_split")
        gate_w_loaded = sem("gate_w_loaded")
        out_done = sem("out_done")
        out_used = sem("out_used")
        conv_ready = sem("conv_ready")
        decay_ready = sem("decay_ready")
        root_ready = sem("root_ready")
        lru_done = sem("lru_done")
        lam_exp = sem("lam_exp")
        lam_ready = sem("lam_ready")
        stage_stored = [sem("stage_stored0"), sem("stage_stored1")]
        att_tables = sem("att_tables")
        fa_turned = sem("fa_turned")
        fa_arg_ready = sem("fa_arg_ready")
        fa_exp_ready = sem("fa_exp_ready")
        fa_ready = sem("fa_ready")
        eps_ready = sem("eps_ready")
        lam_exp_ready = sem("lam_exp_ready")
        y_stored = sem("y_stored")
        logf_ready = sem("logf_ready")
        logf_turned = sem("logf_turned")
        cum_ready = sem("cum_ready")
        cum_stored = sem("cum_stored")
        cum_loaded = sem("cum_loaded")
        bf_loaded = sem("bf_loaded")
        clogf_loaded = sem("clogf_loaded")
        rel_loaded = sem("rel_loaded")
        rel_filled = sem("rel_filled")
        rel_stored = sem("rel_stored")
        rel_skewed = sem("rel_skewed")
        k_loaded = sem("k_loaded")
        v_loaded = [sem("v_loaded0"), sem("v_loaded1")]
        band_v_loaded = sem("band_v_loaded")
        cache_k_loaded = sem("cache_k_loaded")
        cache_v_loaded = sem("cache_v_loaded")
        state_turned = sem("state_turned")
        rows_ready = sem("rows_ready")
        q_blocks_zero = sem("q_blocks_zero")
        q_blocks_ready = sem("q_blocks_ready")
        scores_ready = sem("scores_ready")
        scores_used = sem("scores_used")
        exp_ready = sem("exp_ready")
        probs_ready = sem("probs_ready")
        probs_turned = sem("probs_turned")
        probs_t_ready = sem("probs_t_ready")
        att_out = sem("att_out")
        att_out_used = sem("att_out_used")
        res_loaded = sem("res_loaded")
        mixed = sem("mixed")
        mix_sq = sem("mix_sq")
        x1_ready = sem("x1_ready")
        x1_sq = sem("x1_sq")
        y2_ready = sem("y2_ready")
        y2_turned = sem("y2_turned")
        x1_stored = sem("x1_stored")
        h2_hi = sem("h2_hi")
        h2_lo = sem("h2_lo")
        low_half_mixed = sem("low_half_mixed")
        gate_done = sem("gate_done")
        val_done = sem("val_done")
        gate_evac = sem("gate_evac")
        fconv_ready = sem("fconv_ready")
        gelu_ready = sem("gelu_ready")
        f_ready = sem("f_ready")
        f_hi_ready = sem("f_hi_ready")
        f_lo_ready = sem("f_lo_ready")
        down_done = sem("down_done")
        added = sem("added")
        x1_loaded = sem("x1_loaded")
        f_sq = sem("f_sq")
        f_normed = sem("f_normed")
        y_final = sem("y_final")
        ffn_turned = sem("ffn_turned")
        ffn_rows_ready = sem("ffn_rows_ready")
        stored = sem("stored")

        R_OUT = 2 * NU
        R_FFN = R_OUT + 8
        ZERO_AT = 6
        MIX_AHEAD = 3
        FIRST_SPLITS = (2, 3)

        def mixed_banks(t):
            return 6 if t % 2 == 0 else 2

        def probs_of(r):
            assert COUNT[FIRST["pb"]] % 3 == 0
            if r < COUNT[FIRST["pb"]]:
                return raw[:, 0, 0:1024] if r % 3 == 2 else probs[:, r % 3, :]
            return probs[:, :, :].rearrange("p a b -> p (a b)")[:, BANDW * (r % 3):BANDW * (r % 3 + 1)]

        def turned_x(t):
            b0 = 6 - 2 * (t % 2)
            return PS[:, b0:b0 + 2, :].rearrange("p b (k c) -> p (b k) c", c=P)

        block = ctx.enter_context(nc.Block())

        @block.sync
        def _(sp):
            for t in range(3):
                sp.dma_start(x_in[:, t, :], rows_of(xp, xs, t)).then_inc(x_loaded[t], 16)
                if t == 0:
                    sp.dma_start(gains[:, 0, :], i["norm_g"][0, 0:1, :].to_broadcast([P, D]))\
                      .then_inc(gain_loaded, 16)

            def load_half(r, dst, src):
                if r >= 2:
                    sp.wait_ge(w_lo_ready, r - 1)
                sp.dma_start(dst, src).then_inc(raw_loaded[r % 2], 16)

            def load_in(r):
                c0 = UNITS[r // 2][1]
                k0 = 4 * (r % 2)
                load_half(r, raw[:, r % 2, :].rearrange("p (k c) -> p k c", k=4),
                          w_in[k0 * P:(k0 + 4) * P, c0:c0 + 256].rearrange("(k p) c -> p k c", p=P))

            load_in(0)
            load_in(1)
            for t in range(3, NT):
                sp.wait_ge(y_ready, t - 2)
                sp.dma_start(x_in[:, t % 3, :], rows_of(xp, xs, t)).then_inc(x_loaded[t % 3], 16)
            for r in range(2, 2 * NU):
                load_in(r)
                if r == 4:
                    sp.dma_start(fa_raw[:, :, :], w_in[:, C_FA:C_FA + H].rearrange("(k p) c -> p k c", p=P))\
                      .then_inc(fa_loaded, 16)
            for q in range(8):
                r = R_OUT + q
                h, k0 = q // 4, 2 * (q % 4)
                if q == 0:
                    sp.wait_ge(probs_turned, COUNT[LAST["sf"]] + 1)
                load_half(r, raw[:, r % 2, :].rearrange("p (k c) -> p k c", k=2),
                          w_out[k0 * P:(k0 + 2) * P, h * 512:(h + 1) * 512].rearrange("(k p) c -> p k c", p=P))
            sp.wait_ge(y_ready, NT)
            for g in range(2):
                sp.dma_start(gains[:, g, :], i["norm_g"][0, 1 + g:2 + g, :].to_broadcast([P, D]))\
                  .then_inc(gain2_loaded, 16)

            def load_group_half(g, r0, k):
                sp.wait_ge(w_lo_ready, r0 + k - 1)
                if k < 2 * FG:
                    sp.dma_start(raw[:, k % 2, :].rearrange("p (k c) -> p k c", k=KD),
                                 w_up[:, bass.ds(g * (FG * P) + (k % 2 * DFF + k // 2 * P), P)]
                                 .rearrange("(k p) c -> p k c", p=P)).then_inc(raw_loaded[k % 2], 16)
                else:
                    sp.dma_start(raw[:, k % 2, :], w_down[bass.ds(g * (FG * P) + (k - 2 * FG) * P, P), :])\
                      .then_inc(raw_loaded[k % 2], 16)

            for k in range(2):
                load_group_half(0, R_FFN, k)
            for t in range(NT):
                if t == 0:
                    sp.wait_ge(att_out_used, NREAL)
                else:
                    sp.wait_ge(x1_ready, t)
                sp.dma_start(x_res[:, :], rows_of(xp, xs, t)).then_inc(res_loaded, 16)
            for k in range(2, 6):
                load_group_half(0, R_FFN, k)
            with sp.Fori(1, NG) as g:
                for k in range(6):
                    load_group_half(g, g * 6 + R_FFN, k)
            sp.wait_ge(y2_ready, NT)
            sp.dma_start(gains[:, 0, :], i["norm_g"][0, 3:4, :].to_broadcast([P, D])).then_inc(gain3_loaded, 16)
            sp.wait_ge(x1_stored, 16 * NT)
            sp.wait_ge(val_done, FT)
            sp.dma_start(x1_back[:, :, :], x1_dram.rearrange("(c p) d -> p c d", p=P)).then_inc(x1_loaded, 16)
            for t in range(NT):
                sp.wait_ge(y_final, t + 1)
                sp.dma_start(rows_of(yp, ys, t), f_acc[:, t, :]).then_inc(y_stored, 16)
            sp.wait_ge(y_stored, 16 * NT)

        @block.gpsimd
        def _(pool):
            step = Chain(pool, pool_step)
            step(pool.memset(ident[:, :], 0.0))
            step(pool.affine_select(out=ident[:, :], in_=ident[:, :], compare_op=ALU.not_equal, fill=1.0, base=0,
                                    pattern=[[-1, P]], channel_multiplier=1))
            pool.tensor_copy(ident_b[:, :], ident[:, :]).then_inc(consts_ready, 1)
            step(pool.memset(cmask_b[:, :], 0.0))
            pool.affine_select(out=cmask_b[:, :], in_=cmask_b[:, :], compare_op=ALU.is_ge, fill=BIG, base=0,
                               pattern=[[-1, P]], channel_multiplier=1).then_inc(consts_ready, 1)
            step(pool.memset(chan_rows[:, :, :], 0.0))
            loads = [(0, 0, i["lru_conv_w"].rearrange("l k (j p) -> (l k j) p", p=P)),
                     (0, 16, i["lru_conv_b"].rearrange("l (j p) -> (l j) p", p=P)),
                     (0, 20, i["lru_ba"].rearrange("l (j p) -> (l j) p", p=P)),
                     (0, 24, i["lru_bx"].rearrange("l (j p) -> (l j) p", p=P)),
                     (0, 28, i["lru_lambda"].rearrange("l (j p) -> (l j) p", p=P)),
                     (0, 32, i["state_lru_h"].rearrange("l b (j p) -> (l b j) p", p=P)),
                     (1, 0, i["ffn_conv_w"].rearrange("l k (j p) -> (l k j) p", p=P)),
                     (1, 72, i["ffn_conv_b"].rearrange("l (j p) -> (l j) p", p=P)),
                     (2, 0, i["state_lru_conv"].rearrange("l b k (j p) -> (l b k j) p", p=P))]
            hist = i["state_ffn_conv"].rearrange("l b k (j p) -> (l b k j) p", p=P)
            loads += [(3 + c, 0, hist[c * P:(c + 1) * P, :]) for c in range(3)]
            for slot, row, src in loads:
                pool.dma_start(chan_rows[row:row + src.shape[0], slot, :], src).then_inc(chan_loaded, 16)
            assert len(loads) == 12
            step(pool.memset(gate_w[:, :, :, :], 0.0))
            for k, name in enumerate(("lru_wa", "lru_wx")):
                src = i[name][0].rearrange("(j two) d e -> two d j e", two=2)
                for two in range(2):
                    pool.dma_start(gate_w[64 * two:64 * two + 64, k, :, 64 * two:64 * two + 64], src[two])\
                        .then_inc(gate_w_loaded, 16)
            pool.dma_start(stat[:, BF_:BF_ + H], i["b_forget"].to_broadcast([P, H])).then_inc(bf_loaded, 16)
            for s, lot in enumerate(STORES):
                pool.wait_ge(out_used, KV_OUTS[s] + 1)
                for name, t0, n, c in lot:
                    dst = kv_dram.get(name)
                    if dst is None:
                        dst = kv_out[name]
                    row0 = t0 - (4 if name in ("bk_p", "bv_p") else 0)
                    row0 = 0 if name.endswith("_s") else row0
                    pool.dma_start(tile_rows(dst, row0, n), stage[:, s % 2, c:c + n, :])\
                        .then_inc(stage_stored[s % 2], 16)

            last = len(STORES) - 1
            for q in range(2):
                pool.wait_ge(stage_stored[q], 16 * stores_until(q, last))
            pool.wait_ge(lru_done, LT)
            pool.dma_start(k_rows[:, 0:NPT, :], tile_rows(kv_out["fk_p"], 0, NPT)).then_inc(k_loaded, 16)
            pool.dma_start(k_rows[:, NPT:NT, :], tile_rows(kv_out["fk_s"], 0, 1)).then_inc(k_loaded, 16)
            step(pool.memset(upper[:, :], 1.0))
            pool.affine_select(out=upper[:, :], in_=upper[:, :], compare_op=ALU.is_ge, fill=0.0, base=0,
                               pattern=[[1, SK]], channel_multiplier=-1).then_inc(att_tables, 1)
            blk = stat[:, BLK:BLK + NS]
            step(pool.memset(blk, 1.0))
            step(pool.affine_select(out=blk, in_=blk, compare_op=ALU.is_ge, fill=0.0, base=0,
                                    pattern=[[-TS, NS]], channel_multiplier=1))
            pool.affine_select(out=blk, in_=blk, compare_op=ALU.is_ge, fill=0.0, base=TS - 1,
                               pattern=[[TS, NS]], channel_multiplier=-1).then_inc(att_tables, 1)
            pool.wait_ge(rows_ready, 1)
            for name, r0, n in (("lru_h_p", 0, 1), ("lru_h_s", 1, NS)):
                pool.dma_start(o[name].rearrange("l b c -> (l b) c"), state_rows[r0:r0 + n, :]).then_inc(stored, 16)
            for name, r0, n in (("lru_conv_p", 9, LH), ("lru_conv_s", 12, NS * LH)):
                pool.dma_start(o[name].rearrange("l b k c -> (l b k) c"), state_rows[r0:r0 + n, :]).then_inc(stored, 16)
            pool.wait_ge(logf_ready, 1)
            pool.dma_start(o["fox_logf_p"].rearrange("l b (c p) h -> p (l b c) h", p=P), logf[:, 0:NPT, :])\
                .then_inc(stored, 16)
            pool.dma_start(o["fox_logf_s"].rearrange("l b s h -> (l b s) h"), logf[:, NPT, :]).then_inc(stored, 16)
            pool.wait_ge(cum_ready, 1)
            pool.dma_start(cum_dram, cum_rows).then_inc(cum_stored, 16)
            pool.wait_ge(cum_stored, 16)
            pool.wait_ge(out_done, last_output(NU - 2) + 1)
            pool.dma_start(cum_b[:, :, :], cum_dram.rearrange("(a h) c -> a h c", a=1).to_broadcast([P, H, SEQ]))\
                .then_inc(cum_loaded, 16)
            pool.wait_ge(out_done, NO)
            for t0, n in ((0, 2), (2, NPT - 2)):
                pool.dma_start(v_f[:, t0:t0 + n, :], tile_rows(kv_out["fv_p"], t0, n)).then_inc(v_loaded[t0 > 0], 16)
            pool.dma_start(v_f[:, NPT:NT, :], tile_rows(kv_out["fv_s"], 0, 1)).then_inc(v_loaded[1], 16)
            pool.memset(q_blocks[:, :, :, :], 0.0).then_inc(q_blocks_zero, 1)
            future = logf_new[:, 0:2, :].rearrange("p a c -> p (a c)").rearrange("p (g c) -> p g c", g=NS)
            step(pool.memset(future, BIG))
            pool.affine_select(out=future, in_=future, compare_op=ALU.is_gt, fill=0.0, base=0,
                               pattern=[[TS, NS], [1, TS]], channel_multiplier=-1).then_inc(att_tables, 1)
            pool.dma_start(cache_logf[:, :, :].rearrange("p (b k) h -> p b k h", k=2),
                           i["cache_fox_logf"][0].rearrange("b (k p) h -> p b k h", p=P)).then_inc(clogf_loaded, 16)
            pool.wait_ge(scores_ready, 3)
            pool.dma_start(rel_rows[:, :, 127:127 + NREL],
                           i["rel_bias"][0:1, :, :].to_broadcast([P, H, NREL])).then_inc(rel_loaded, 16)
            pool.wait_ge(rel_filled, 1)
            pool.dma_start(rel_dram.ap(), k_rows[:, 0:6, :].rearrange("p a b -> p (a b)")).then_inc(rel_stored, 16)
            pool.wait_ge(rel_stored, 16)
            pitch = H * 384
            skewed = bass.AP(rel_dram, 127, [[pitch - 1, P], [384, H], [1, 256]])
            pool.dma_start(k_rows[:, :, :], tile_rows(kv_dram["bk_scr"], 0, NT)).then_inc(k_loaded, 16)
            pool.dma_start(band_bias[:, :, BANDW - 256:], skewed).then_inc(rel_skewed, 16)
            for b2 in range(2):
                for h in range(H):
                    src = bass.AP(rel_dram, 127 + h * 384, [[pitch - 1, TS], [1, P + TS]])
                    row = 64 * b2 + TS * h
                    pool.dma_start(band_bias_s[row:row + TS, P:SK], src).then_inc(rel_skewed, 16)

            def load_cache_k(name):
                src = i[name][0].rearrange("b (k p) h d -> p b k (h d)", p=P)
                for half, dst in enumerate((cache_k_low, cache_k_high)):
                    pool.dma_start(dst[:, :, :, :], src[:, 4 * half:4 * half + 4]).then_inc(cache_k_loaded, 16)

            def load_cache_v(name):
                src = i[name][0].rearrange("b (k p) h d -> p b k (h d)", p=P)
                for half in range(2):
                    pool.dma_start(cache_v[:, 4 * half:4 * half + 4, :, :], src[:, 4 * half:4 * half + 4])\
                        .then_inc(cache_v_loaded, 16)

            load_cache_k("cache_fox_k")
            load_cache_v("cache_fox_v")
            pool.dma_start(v_b[:, :, :], tile_rows(kv_dram["bv_scr"], 0, NT)).then_inc(band_v_loaded, 16)
            pool.wait_ge(scores_ready, KEY_TURNS[NS // 2 - 1] + 1)
            load_cache_k("cache_band_k")
            pool.wait_ge(att_out, COUNT[LAST["sf"]] + 1)
            load_cache_v("cache_band_v")

            for t in range(NT):
                pool.wait_ge(x1_ready, t + 1)
                pool.dma_start(x1_dram[t * P:(t + 1) * P, :], x1[:, :]).then_inc(x1_stored, 16)
                if t == ZERO_AT:
                    pool.wait_ge(lo_ready, 2 * NT)
                    for q in range(2 * NT):
                        pool.memset(f_acc[:, q // 2, (q % 2) * 512:(q % 2 + 1) * 512], 0.0).then_inc(added, 1)
            pool.wait_ge(x1_loaded, 16)
            for t in range(NT):
                pool.wait_ge(f_normed, t + 1)
                pool.tensor_tensor(f_acc[:, t, :], f_acc[:, t, :], x1_back[:, t, :], ALU.add).then_inc(y_final, 1)
            pool.wait_ge(ffn_rows_ready, 6)
            pool.dma_start(o["ffn_conv_p"].rearrange("l b k c -> (l b k) c"), ffn_rows[0:FH, :]).then_inc(stored, 16)
            pool.dma_start(o["ffn_conv_s"].rearrange("l b k c -> (l b k) c"), ffn_rows[FH:18, :]).then_inc(stored, 16)
            pool.wait_ge(stored, 16 * 8)

        @block.scalar
        def _(act):
            step = Chain(act, act_step)

            def norm_hi(t):
                act.wait_ge(x_turned, t + 1)
                act.activation(act_hi[:, :, t * P:(t + 1) * P], turned_x(t), ACT.Copy).then_inc(hi_ready, 1)

            def split_hi(r, dst):
                act.wait_ge(raw_loaded[r % 2], 16 * (r // 2 + 1))
                act.activation(dst, raw[:, r % 2, :], ACT.Copy).then_inc(w_hi_ready, 1)

            def split_unit_half(u, half):
                split_hi(2 * u + half, w_hi[:, u % 3, half * 1024:(half + 1) * 1024])

            act.wait_ge(eps_ready, 1)
            act.activation(stat[:, TMP:TMP + 1], stat[:, EPSC:EPSC + 1], ACT.Sqrt)
            for t in range(NT):
                act.wait_ge(x_loaded[t % 3], 16 * (t // 3 + 1))
                step(act.activation(square0[:, :], x_in[:, t % 3, :], ACT.Square,
                                    accum_out=stat[:, SS0 + t:SS0 + t + 1]))
                act.activation(stat[:, RM0 + t:RM0 + t + 1], stat[:, SS0 + t:SS0 + t + 1], ACT.Sqrt,
                               scale=1.0 / D, bias=stat[:, EPSC:EPSC + 1]).then_inc(rms_ready, 1)
                if t >= 1:
                    norm_hi(t - 1)
                if t in FIRST_SPLITS:
                    split_unit_half(0, FIRST_SPLITS.index(t))
            norm_hi(NT - 1)

            def split_unit(u):
                if u >= 3:
                    act.wait_ge(out_done, last_output(u - 3) + 1)
                for half in range(2):
                    split_unit_half(u, half)

            for u in range(1, 3):
                split_unit(u)
            act.wait_ge(fa_loaded, 16)
            act.activation(fa_hi[:, :, :], fa_raw[:, :, :], ACT.Copy).then_inc(fa_split, 1)
            staged = 0
            for n, (kind, u, j) in enumerate(OUTS):
                banks = PS[:, 3 * (n % 2):3 * (n % 2) + 3, :]
                if kind == "x":
                    act.wait_ge(out_done, n + 1)
                    act.activation(mix[:, MIX_OF_X[j], :].rearrange("p (b c) -> p b c", b=3), banks[:, :, 0:CW],
                                   ACT.Copy).then_inc(out_used, 1)
                    if j == 0:
                        act.wait_ge(chan_turned, 1)
                        act.activation(chan[:, 0:4, :].rearrange("p s c -> p (s c)"), PS[:, 6, :], ACT.Copy)\
                           .then_inc(chan_ready, 1)
                        act.activation(chan[:, 4:6, :].rearrange("p s c -> p (s c)"), PS[:, 7, 0:256], ACT.Copy)\
                           .then_inc(chan_ready, 1)
                        act.wait_ge(lam_exp, 1)
                        act.activation(stat[:, TMP + LT:TMP + 2 * LT], stat[:, TMP:TMP + LT], ACT.Exp, scale=-1.0)\
                           .then_inc(lam_exp_ready, 1)
                elif kind == "y":
                    act.wait_ge(out_done, n + 1)
                    act.activation(mix[:, 2 + j, :].rearrange("p (b c) -> p b c", b=3), banks[:, :, 0:CW],
                                   ACT.Gelu_apprx_tanh).then_inc(out_used, 1)
                elif kind in ("gate_r", "gate_i"):
                    if kind == "gate_r" and j >= 1:
                        act.wait_ge(lru_done, j)
                    act.wait_ge(out_done, n + 1)
                    if kind == "gate_r" and j == 0:
                        act.wait_ge(chan_ready, 2)
                    g = 0 if kind == "gate_r" else 1
                    act.activation((gate_r, gate_i)[g][:, :].rearrange("p (b c) -> p b c", b=3),
                                   banks[:, :, 0:LW // 3], ACT.Sigmoid, bias=lru_const(5 + g, j)).then_inc(out_used, 1)
                    if g:
                        act.wait_ge(out_used, n + 1)
                        if j == 0:
                            act.wait_ge(lam_ready, 2)
                        step(act.activation(xpad[:, 0:LW], gate_r[:, :], ACT.Tanh, scale=stat[:, SP4 + j:SP4 + j + 1]))
                        act.activation(gate_r[:, :], gate_r[:, :], ACT.Exp, scale=stat[:, SP8 + j:SP8 + j + 1])\
                           .then_inc(decay_ready, 1)
                        act.activation(xpad[:, 0:LW], xpad[:, 0:LW], ACT.Sqrt).then_inc(root_ready, 1)
                elif kind in KV:
                    if staged >= 2:
                        act.wait_ge(stage_stored[staged % 2], 16 * stores_until(staged % 2, staged - 2))
                    act.wait_ge(out_done, n + 1)
                    act.activation(stage[:, staged % 2, :, :], banks[:, :, 0:DH], ACT.Copy).then_inc(out_used, 1)
                    staged += 1
                elif kind in ("fq", "bq"):
                    act.wait_ge(conv_ready, LT)
                    act.wait_ge(out_done, n + 1)
                    act.activation(mix[:, (0 if kind == "fq" else 6) + j, :].rearrange("p (b c) -> p b c", b=3),
                                   banks[:, :, 0:CW], ACT.Copy, scale=QS).then_inc(out_used, 1)
                    if kind == "fq" and j == 0:
                        act.wait_ge(state_turned, 1)
                        act.activation(state_rows[0:36, :], PS[0:36, 7, :], ACT.Copy).then_inc(rows_ready, 1)
                        act.wait_ge(fa_arg_ready, 1)
                        act.activation(stat[:, TMP + 72:TMP + 108], stat[:, TMP + 36:TMP + 72], ACT.Exp, scale=-1.0)\
                           .then_inc(fa_exp_ready, 1)
                elif kind == "fa":
                    act.wait_ge(lru_done, LT)
                    act.wait_ge(out_done, n + 1)
                    act.activation(fa_rows.rearrange("p (b c) -> p b c", b=3), banks[0:H, :, 0:CW], ACT.Copy)\
                       .then_inc(out_used, 1)
                if u is not None and n == last_output(u) and u + 3 < NU:
                    split_unit(u + 3)

            def widths(n):
                st = STEPS[n]
                return SK if st[0][0] == "s" else P * key_blocks(st)[1]

            def turned_back(r):
                n = REAL[r]
                act.wait_ge(probs_turned, r + 1)
                if r >= 2:
                    act.wait_ge(att_out, r - 1)
                if r == 1:
                    act.wait_ge(stored, 16 * 6)
                w = 3 * P if STEPS[n][0][0] == "s" else widths(n)
                act.activation(probs_t[:, r % 2, 0:w], PS[:, 4:6, :].rearrange("p b c -> p (b c)")[:, 0:w], ACT.Copy)\
                   .then_inc(probs_t_ready, 1)

            def out_split(q):
                if q == 0:
                    act.wait_ge(att_out, COUNT[LAST["sb"]] + 1)
                split_hi(R_OUT + q, w_hi[:, q // 2, (q % 2) * 1024:(q % 2 + 1) * 1024])

            for r, n in enumerate(REAL):
                if r >= 2:
                    turned_back(r - 2)
                act.wait_ge(scores_used, n + 1)
                p_r = probs_of(r)[:, 0:widths(n)]
                act.activation(p_r, p_r, ACT.Exp, scale=-1.0, bias=stat[:, RMIN + r % 4:RMIN + r % 4 + 1],
                               accum_out=stat[:, RSUM + r % 4:RSUM + r % 4 + 1]).then_inc(exp_ready, 1)
                if n in OUT_SPLITS:
                    out_split(OUT_SPLITS.index(n))
            turned_back(NREAL - 2)
            turned_back(NREAL - 1)

            act.wait_ge(att_out_used, NREAL)

            def mix_hi(t):
                act.activation(act_hi[:, :, t * P:(t + 1) * P], mix[:, :, t * P:(t + 1) * P], ACT.Copy)\
                   .then_inc(hi_ready, 1)

            mix_hi(0)
            for q in (6, 7):
                split_hi(R_OUT + q, wx_hi[:, (q - 6) * 1024:(q - 5) * 1024])
            for t in range(1, MIX_AHEAD):
                mix_hi(t)

            def split_group_half(q, k):
                act.wait_ge(raw_loaded[k % 2], q)
                act.activation(w_hi[:, k // 2, (k % 2) * 1024:(k % 2 + 1) * 1024], raw[:, k % 2, :], ACT.Copy)\
                   .then_inc(w_hi_ready, 1)

            def landed(g, k):
                return (g * 3 + (R_FFN // 2 + k // 2 + 1)) * 16

            def h2_half(t):
                act.wait_ge(y2_turned, t + 1)
                act.activation(act_hi[:, :, t * P:(t + 1) * P],
                               PS[:, 4:6, :].rearrange("p b (k c) -> p (b k) c", c=P), ACT.Copy).then_inc(h2_hi, 1)

            for t in range(NT):
                s0 = mixed_banks(t)
                if t + MIX_AHEAD < NT:
                    mix_hi(t + MIX_AHEAD)
                if t == NT - 1:
                    act.wait_ge(low_half_mixed, 1)
                    for k in range(2):
                        split_group_half(landed(0, k), k)
                if t >= 1:
                    act.wait_ge(x1_stored, 16 * t)
                    act.wait_ge(y2_ready, t)
                act.wait_ge(mixed, t + 1)
                step(act.activation(x1[:, :], PS[:, s0:s0 + 2, :].rearrange("p b c -> p (b c)"), ACT.Square,
                                    accum_out=stat[:, SS1 + t:SS1 + t + 1]))
                act.activation(stat[:, SS1 + t:SS1 + t + 1], stat[:, SS1 + t:SS1 + t + 1], ACT.Sqrt, scale=1.0 / D,
                               bias=stat[:, EPSC:EPSC + 1]).then_inc(mix_sq, 1)
                if t >= 1:
                    h2_half(t - 1)
                act.wait_ge(x1_ready, t + 1)
                step(act.activation(y2[:, :], x1[:, :], ACT.Square, accum_out=stat[:, SS2 + t:SS2 + t + 1]))
                act.activation(stat[:, SS2 + t:SS2 + t + 1], stat[:, SS2 + t:SS2 + t + 1], ACT.Sqrt, scale=1.0 / D,
                               bias=stat[:, EPSC:EPSC + 1]).then_inc(x1_sq, 1)
            h2_half(NT - 1)

            for k in range(2, 6):
                split_group_half(landed(0, k), k)
            act.wait_ge(x1_stored, 16 * NT)

            def ffn_tile(j, c):
                if c:
                    act.wait_ge(f_lo_ready, j)
                act.wait_ge(gate_done, j + 1)
                act.activation(gate_pad[:, FH:FH + 2 * CW].rearrange("p (b c) -> p b c", b=2), PS[:, 0:2, 0:CW],
                               ACT.Copy)
                act.activation(gate_pad[:, FH + 2 * CW:FH + SEQ], PS[:, 2, 0:SEQ - 2 * CW], ACT.Copy)
                act.activation(gate_pad[:, FH + SEQ:].rearrange("p (b c) -> p b c", b=NS)[:, :, FH:],
                               PS[:, 2, SEQ - 2 * CW:CW].rearrange("p (b c) -> p b c", b=NS), ACT.Copy)\
                   .then_inc(gate_evac, 1)
                act.wait_ge(fconv_ready, j + 1)
                act.activation(gate_conv[:, :], gate_conv[:, :], ACT.Gelu_apprx_tanh).then_inc(gelu_ready, 1)

            def ffn_hi(j, c):
                act.wait_ge(f_ready, j + 1)
                act.activation(f_hi[:, c, :], gate_pad[:, FH:FH + T], ACT.Copy).then_inc(f_hi_ready, 1)

            def ffn_group(g, more):
                for c in range(FG):
                    ffn_tile(g * FG + c, c)
                    ffn_hi(g * FG + c, c)
                    if more:
                        act.wait_ge(val_done, g * FG + (c + 1))
                        for half in range(2):
                            split_group_half(landed(g + 1, 2 * c + half), 2 * c + half)
                if more:
                    act.wait_ge(down_done, g * 18 + 18)
                    for k in range(4, 6):
                        split_group_half(landed(g + 1, k), k)

            with act.Fori(0, NG - 1) as g:
                ffn_group(g, True)
            ffn_group(NG - 1, False)
            def state_rows_out(c):
                act.wait_ge(ffn_turned, c + 1)
                act.activation(ffn_rows[:, c * 512:(c + 1) * 512], PS[0:18, bank_of(8 + c), :], ACT.Copy)\
                   .then_inc(ffn_rows_ready, 1)

            for t in range(NT):
                for c in range(6):
                    if t == (7 + c) // 2:
                        state_rows_out(c)
                act.wait_ge(added, 18 * NG + 2 * t + 2)
                step(act.activation(square3[:, :], f_acc[:, t, :], ACT.Square,
                                    accum_out=stat[:, SS3 + t:SS3 + t + 1]))
                act.activation(stat[:, SS3 + t:SS3 + t + 1], stat[:, SS3 + t:SS3 + t + 1], ACT.Sqrt, scale=1.0 / D,
                               bias=stat[:, EPSC:EPSC + 1]).then_inc(f_sq, 1)

        @block.vector
        def _(dve):
            step = Chain(dve, dve_step)

            def subtract(out, a, hi):
                return dve.tensor_tensor(out, a, hi.bitcast(F32), ALU.subtract)

            def softplus_of_minus(out, z, e, n, tmp):
                q, q2, s = (stat[:, tmp + k * n:tmp + (k + 1) * n] for k in range(3))
                step(dve.tensor_scalar(q, e, 2.0, None, ALU.add))
                step(dve.reciprocal(q, q))
                step(dve.tensor_tensor(q, q, e, ALU.mult))
                step(dve.tensor_tensor(q2, q, q, ALU.mult))
                step(dve.tensor_scalar(s, q2, 1.0 / 17, None, ALU.mult))
                for k in (15, 13, 11, 9, 7, 5, 3):
                    step(dve.scalar_tensor_tensor(s, s, 1.0 / k, q2, ALU.add, ALU.mult))
                step(dve.scalar_tensor_tensor(s, s, 1.0, q, ALU.add, ALU.mult))
                step(dve.tensor_scalar(q, z, -1.0, 0.0, ALU.mult, ALU.max))
                return dve.scalar_tensor_tensor(out, s, 2.0, q, ALU.mult, ALU.add)

            def norm_lo(t):
                dve.wait_ge(hi_ready, t + 1)
                cols = slice(t * P, (t + 1) * P)
                subtract(act_lo[:, :, cols], turned_x(t), act_hi[:, :, cols]).then_inc(lo_ready, 1)

            def split_lo(r, hi, lo):
                dve.wait_ge(w_hi_ready, r + 1)
                subtract(lo, raw[:, r % 2, :], hi).then_inc(w_lo_ready, 1)

            def split_unit_half(u, half):
                cols = slice(half * 1024, (half + 1) * 1024)
                split_lo(2 * u + half, w_hi[:, u % 3, cols], w_lo[:, u % 3, cols])

            dve.memset(stat[:, EPSC:EPSC + 1], EPS).then_inc(eps_ready, 1)
            dve.wait_ge(gain_loaded, 16)
            for t in range(NT):
                dve.wait_ge(rms_ready, t + 1)
                step(dve.reciprocal(stat[:, RR0 + t:RR0 + t + 1], stat[:, RM0 + t:RM0 + t + 1]))
                if t >= 2:
                    dve.wait_ge(x_turned, t - 1)
                dve.scalar_tensor_tensor(y_in[:, t % 2, :], x_in[:, t % 3, :], stat[:, RR0 + t:RR0 + t + 1],
                                         gains[:, 0, :], ALU.mult, ALU.mult).then_inc(y_ready, 1)
                if t >= 1:
                    norm_lo(t - 1)
                if t in FIRST_SPLITS:
                    split_unit_half(0, FIRST_SPLITS.index(t))
            norm_lo(NT - 1)

            def split_unit(u):
                for half in range(2):
                    split_unit_half(u, half)

            pitch = LH + TS

            def lru_conv(j):
                x = mix[:, MIX_OF_X[j], :]
                dve.wait_ge(out_used, OUTS.index(("x", j // 2, j)) + 1)
                dve.memset(xpad[:, 0:LH], 0.0)
                dve.tensor_copy(xpad[:, LH:LH + SEQ], x[:, 0:SEQ])
                pads = xpad[:, LH + SEQ:LPAD].rearrange("p (b c) -> p b c", b=NS)
                news = x[:, SEQ:T].rearrange("p (b c) -> p b c", b=NS)
                dve.tensor_copy(pads[:, :, LH:], news)
                dve.tensor_copy(pads[:, :, 0:LH], lru_hist[:, :, :, j])
                dve.tensor_copy(lru_state[:, j, 9:9 + LH], x[:, SEQ - LH:SEQ])
                step(dve.tensor_copy(lru_state[:, j, 12:36].rearrange("p (b k) -> p b k", b=NS), news[:, :, TS - LH:]))
                step(dve.tensor_scalar(xconv[:, :], xpad[:, 0:LW], lru_const(0, j), lru_const(4, j), ALU.mult, ALU.add))
                for k in range(1, LCONV):
                    ins = dve.scalar_tensor_tensor(xconv[:, :], xpad[:, k:k + LW], lru_const(k, j), xconv[:, :],
                                                   ALU.mult, ALU.add)
                    if k < LCONV - 1:
                        step(ins)
                ins.then_inc(conv_ready, 1)

            def lru_scan(j):
                dve.wait_ge(decay_ready, j + 1)
                step(dve.tensor_tensor(gate_i[:, :], gate_i[:, :], xconv[:, :], ALU.mult))
                step(dve.scalar_tensor_tensor(gate_i[:, :], gate_r[:, :], 1.0, gate_i[:, :], ALU.add, ALU.mult))
                dve.wait_ge(root_ready, j + 1)
                step(dve.tensor_tensor(gate_i[:, :], gate_i[:, :], xpad[:, 0:LW], ALU.mult))
                starts = slice(SEQ + LH - 1, SEQ + LH - 1 + pitch * (NS - 1) + 1, pitch)
                dve.memset(gate_r[:, starts], 0.0)
                step(dve.tensor_copy(gate_i[:, starts], h0[:, :, j]))
                step(dve.tensor_tensor_scan(xconv[:, :], gate_r[:, :], gate_i[:, :], 0.0, ALU.mult, ALU.add))
                first = SEQ + LH
                y = mix[:, 2 + j, :]
                dve.wait_ge(out_used, OUTS.index(("y", 2 + j // 2, j)) + 1)
                dve.tensor_tensor(y[:, 0:SEQ], y[:, 0:SEQ], xconv[:, 0:SEQ], ALU.mult)
                ys_ = y[:, SEQ:T].rearrange("p (b c) -> p b c", b=NS)
                last = first + (NS - 1) * pitch
                dve.tensor_tensor(ys_[:, 0:NS - 1, :], ys_[:, 0:NS - 1, :],
                                  xconv[:, first:last].rearrange("p (b c) -> p b c", c=pitch)[:, :, 0:TS], ALU.mult)
                dve.tensor_tensor(ys_[:, NS - 1, :], ys_[:, NS - 1, :], xconv[:, last:last + TS], ALU.mult)
                dve.tensor_copy(lru_state[:, j, 0:1], xconv[:, SEQ - 1:SEQ])
                dve.tensor_copy(lru_state[:, j, 1:9], xconv[:, first + TS - 1:last + TS:pitch]).then_inc(lru_done, 1)

            for u in range(1, 3):
                split_unit(u)
            dve.wait_ge(fa_split, 1)
            subtract(fa_lo[:, :, :], fa_raw[:, :, :], fa_hi[:, :, :]).then_inc(fa_ready, 1)
            dve.wait_ge(chan_ready, 2)
            dve.scalar_tensor_tensor(stat[:, TMP:TMP + LT], lam, -1.0, lam, ALU.mult, ALU.max).then_inc(lam_exp, 1)
            dve.wait_ge(lam_exp_ready, 1)
            step(softplus_of_minus(stat[:, SP4:SP4 + LT], lam, stat[:, TMP + LT:TMP + 2 * LT], LT, TMP + 2 * LT))
            dve.tensor_scalar(stat[:, SP8:SP8 + LT], stat[:, SP4:SP4 + LT], -8.0, None, ALU.mult).then_inc(lam_ready, 1)
            dve.wait_ge(lam_ready, 1)
            dve.tensor_scalar(stat[:, SP4:SP4 + LT], stat[:, SP4:SP4 + LT], 4.0, None, ALU.mult).then_inc(lam_ready, 1)
            lru_conv(0)
            split_unit(3)
            split_unit(4)
            for j in range(LT):
                lru_scan(j)
                if j < LT - 1:
                    split_unit(5 + j)
                    lru_conv(j + 1)
            for u in range(8, NU):
                split_unit(u)

            z, az, e = (stat[:, TMP + 36 * k:TMP + 36 * (k + 1)] for k in range(3))
            dve.wait_ge(bf_loaded, 16)
            dve.wait_ge(fa_turned, 1)
            bf = stat[:, BF_:BF_ + H].rearrange("p (a h) -> p a h", a=1).to_broadcast([P, NT, H])
            step(dve.tensor_tensor(z.rearrange("p (t h) -> p t h", h=H),
                                   PS[:, 6, 0:NT * H].rearrange("p (t h) -> p t h", h=H), bf, ALU.add))
            dve.scalar_tensor_tensor(az, z, -1.0, z, ALU.mult, ALU.max).then_inc(fa_arg_ready, 1)
            dve.wait_ge(fa_exp_ready, 1)
            step(softplus_of_minus(az, z, e, 36, TMP + 36 * 3))
            dve.tensor_scalar(logf[:, :, :].rearrange("p t h -> p (t h)"), az, -1.0, None, ALU.mult)\
               .then_inc(logf_ready, 1)
            step(dve.memset(one_rows, 1.0))
            dve.wait_ge(logf_turned, 1)
            dve.tensor_tensor_scan(cum_rows, one_rows, PS[0:H, 6:8, :].rearrange("p b c -> p (b c)"), 0.0,
                                   ALU.mult, ALU.add).then_inc(cum_ready, 1)

            def spread_queries(tile0):
                dve.wait_ge(q_blocks_zero, 1)
                for h in range(H):
                    t, rows = h // 2, slice(64 * (h % 2), 64 * (h % 2) + 64)
                    last = dve.tensor_copy(q_blocks[rows, :, t, TS * h:TS * (h + 1)],
                                           mix[rows, tile0 + t, SEQ:T].rearrange("p (b c) -> p b c", b=NS))
                last.then_inc(q_blocks_ready, 1)

            def new_frames_mask():
                dve.wait_ge(att_tables, 3)
                blk = stat[:, BLK:BLK + NS]
                future = logf_new[:, 0:2, :].rearrange("p a c -> p (a c)").rearrange("p (g c) -> p g c", g=NS)
                step(dve.memset(fox_mask_s[:, 0:PAST], 0.0))
                step(dve.tensor_tensor(future, future, blk.rearrange("p (g a) -> p g a", a=1).to_broadcast([P, NS, TS]),
                                       ALU.mult))
                step(dve.tensor_reduce(fox_mask_s[:, PAST:SK], future.rearrange("p g c -> p c g"), AX.X, ALU.add))

            def forget_rows():
                blk = stat[:, BLK:BLK + NS]
                new = logf[:, NPT, :].rearrange("p (h a) -> p h a", a=1).to_broadcast([P, H, TS])
                for b in range(NS):
                    dve.tensor_scalar(logf_new[:, b, :].rearrange("p (h c) -> p h c", h=H), new, blk[:, b:b + 1], None,
                                      ALU.mult)
                dve.wait_ge(clogf_loaded, 16)
                dve.tensor_copy(logf_rows[:, :, :].rearrange("p k (h c) -> p (k h) c", h=H),
                                cache_logf[:, :, :].rearrange("p k (h a) -> p (k h) a", a=1)
                                .to_broadcast([P, 2 * NS * H, TS]))

            def fill_rel():
                dve.wait_ge(rel_loaded, 16)
                dve.memset(rel_rows[:, :, 127 + NREL:384], 0.0)
                dve.tensor_copy(rel_rows[:, :, 0:127], rel_rows[:, :, 127:128].to_broadcast([P, H, 127]))\
                   .then_inc(rel_filled, 1)

            def band_tables():
                dve.wait_ge(rel_skewed, 16 * (1 + 2 * H))
                step(dve.tensor_scalar(band_bias[:, :, BANDW - 256:], band_bias[:, :, BANDW - 256:], -1.0, None,
                                       ALU.mult))
                step(dve.tensor_copy(band_bias[:, :, 0:BANDW - 256],
                                     band_bias[:, :, BANDW - 256:BANDW - 255].to_broadcast([P, H, BANDW - 256])))
                dve.memset(band_bias[0:64, :, BANDW - CHUNK:], BIG)
                dve.memset(band_bias[64:P, :, 0:CHUNK], BIG)
                step(dve.tensor_scalar(band_bias_s[:, P:SK], band_bias_s[:, P:SK], -1.0, None, ALU.mult))
                step(dve.tensor_copy(band_bias_s[:, 0:P], band_bias_s[:, P:P + 1].to_broadcast([P, P])))

            def take_scores(n):
                st, s = STEPS[n], n % 2
                src = PS[:, 2 * s:2 * s + 2, :].rearrange("p b c -> p (b c)")
                dve.wait_ge(scores_ready, n + 1)
                if st[0] == "kt":
                    dve.tensor_copy(kt_s[:, 2 * st[1]:2 * st[1] + 2, :, :].rearrange("p b t c -> p (b t c)"), src)\
                        .then_inc(scores_used, 1)
                    return
                if st[0][0] == "k":
                    kt = kt_f if st[0] == "kf" else kt_b
                    if st[1] < 2:
                        ins = dve.tensor_copy(kt[:, st[1], 0:SEQ], src)
                    else:
                        ins = dve.tensor_copy(kt[:, :, SEQ:T], src[:, 0:2 * P].rearrange("p (t c) -> p t c", t=2))
                    ins.then_inc(scores_used, 1)
                    return
                r = COUNT[n]
                if r == 0:
                    dve.wait_ge(cum_loaded, 16)
                if st[0] == "sf":
                    w, bias = SK, fox_mask_s[:, :]
                elif st[0] == "sb":
                    w, bias = SK, band_bias_s[:, :]
                elif st[0] == "pf":
                    w = P * key_blocks(st)[1]
                    bias = cum_b[:, st[1], 0:w]
                else:
                    w = P * key_blocks(st)[1]
                    bias = band_bias[:, st[1], BANDW - w:BANDW]
                if r >= 3:
                    dve.wait_ge(probs_turned, r - 2)
                dve.tensor_tensor_reduce(out=probs_of(r)[:, 0:w], in0=src[:, 0:w], in1=bias, scale=1.0, scalar=START,
                                         op0=ALU.add, op1=ALU.min,
                                         accum_out=stat[:, RMIN + r % 4:RMIN + r % 4 + 1]).then_inc(scores_used, 1)

            def normalise(r):
                st, s, p_r = STEPS[REAL[r]], r % 2, probs_of(r)
                inv = stat[:, RINV + s:RINV + s + 1]
                if st[0][0] == "s":
                    step(dve.memset(p_r[:, 512:512 + P], 0.0))
                dve.wait_ge(exp_ready, r + 1)
                step(dve.reciprocal(inv, stat[:, RSUM + r % 4:RSUM + r % 4 + 1]))
                if st[0][0] == "s":
                    for b2 in range(2):
                        rows, c0 = slice(64 * b2, 64 * b2 + 64), 512 + TS * (2 * st[1] + b2)
                        dve.tensor_scalar(p_r[rows, c0:c0 + TS], p_r[rows, PAST:SK],
                                          stat[rows, RINV + s:RINV + s + 1], None, ALU.mult)
                    w = PAST
                else:
                    w = P * key_blocks(st)[1]
                dve.tensor_scalar(p_r[:, 0:w], p_r[:, 0:w], inv, None, ALU.mult).then_inc(probs_ready, 1)

            def take_output(r):
                st, bank = STEPS[REAL[r]], 6 + r % 2
                dve.wait_ge(att_out, r + 1)
                if st[0][0] == "s":
                    tile0 = 0 if st[0] == "sf" else 6
                    for h in range(H):
                        t, rows = h // 2, slice(64 * (h % 2), 64 * (h % 2) + 64)
                        c0 = SEQ + 2 * TS * st[1]
                        last = dve.tensor_copy(
                            mix[rows, tile0 + t, c0:c0 + 2 * TS].rearrange("p (b c) -> p b c", b=2),
                            PS[rows, bank, 128 * t:128 * t + 128].rearrange("p (b c) -> p b c", b=2)
                            [:, :, TS * h:TS * (h + 1)])
                    last.then_inc(att_out_used, 1)
                else:
                    h, q = st[1], st[2]
                    rows = slice(64 * (h % 2), 64 * (h % 2) + 64)
                    dve.tensor_copy(mix[rows, (0 if st[0] == "pf" else 6) + h // 2, q * P:(q + 1) * P],
                                    PS[rows, bank, 0:P]).then_inc(att_out_used, 1)

            take_scores(0)
            take_scores(1)
            for n in range(NSTEP):
                if n in COUNT:
                    normalise(COUNT[n])
                if n + 2 < NSTEP:
                    take_scores(n + 2)
                if n in COUNT and COUNT[n] >= 2:
                    take_output(COUNT[n] - 2)
                if n == REL_FILL_AT:
                    fill_rel()
                if n in SAMPLE_TABLES_AT:
                    (new_frames_mask, forget_rows, lambda: spread_queries(0))[SAMPLE_TABLES_AT.index(n)]()
                if n == BAND_TABLES_AT:
                    band_tables()
                if n == FIRST["pb"] + 2:
                    spread_queries(6)
                if n in OUT_SPLITS:
                    q = OUT_SPLITS.index(n)
                    cols = slice((q % 2) * 1024, (q % 2 + 1) * 1024)
                    split_lo(R_OUT + q, w_hi[:, q // 2, cols], w_lo[:, q // 2, cols])
            take_output(NREAL - 2)
            take_output(NREAL - 1)

            def mix_lo(t):
                cols = slice(t * P, (t + 1) * P)
                dve.wait_ge(hi_ready, NT + t + 1)
                subtract(act_lo[:, :, cols], mix[:, :, cols], act_hi[:, :, cols]).then_inc(lo_ready, 1)

            mix_lo(0)
            for q in (6, 7):
                half = slice((q - 6) * 1024, (q - 5) * 1024)
                split_lo(R_OUT + q, wx_hi[:, half], wx_lo[:, half])
            for t in range(1, MIX_AHEAD):
                mix_lo(t)
            dve.wait_ge(gain2_loaded, 32)

            def split_group_half(r, k):
                cols = slice((k % 2) * 1024, (k % 2 + 1) * 1024)
                dve.wait_ge(w_hi_ready, r + 1)
                subtract(w_lo[:, k // 2, cols], raw[:, k % 2, :], w_hi[:, k // 2, cols]).then_inc(w_lo_ready, 1)

            def h2_lo_half(t):
                cols = slice(t * P, (t + 1) * P)
                dve.wait_ge(h2_hi, t + 1)
                subtract(act_lo[:, :, cols], PS[:, 4:6, :].rearrange("p b (k c) -> p (b k) c", c=P), act_hi[:, :, cols])\
                    .then_inc(h2_lo, 1)

            for t in range(NT):
                if t + MIX_AHEAD < NT:
                    mix_lo(t + MIX_AHEAD)
                if t == NT - 1:
                    for k in range(2):
                        split_group_half(R_FFN + k, k)
                s0 = mixed_banks(t)
                dve.wait_ge(mix_sq, t + 1)
                inv = stat[:, SS1 + t:SS1 + t + 1]
                step(dve.reciprocal(inv, inv))
                step(dve.scalar_tensor_tensor(x1[:, :], PS[:, s0:s0 + 2, :].rearrange("p b c -> p (b c)"), inv,
                                              gains[:, 0, :], ALU.mult, ALU.mult))
                dve.wait_ge(res_loaded, 16 * (t + 1))
                dve.tensor_tensor(x1[:, :], x1[:, :], x_res[:, :], ALU.add).then_inc(x1_ready, 1)
                if t >= 1:
                    h2_lo_half(t - 1)
                dve.wait_ge(x1_sq, t + 1)
                inv = stat[:, SS2 + t:SS2 + t + 1]
                step(dve.reciprocal(inv, inv))
                dve.scalar_tensor_tensor(y2[:, :], x1[:, :], inv, gains[:, 1, :], ALU.mult, ALU.mult)\
                   .then_inc(y2_ready, 1)
            h2_lo_half(NT - 1)

            for k in range(2, 6):
                split_group_half(R_FFN + k, k)
            dve.wait_ge(added, 2 * NT)
            dve.wait_ge(x1_stored, 16 * NT)
            step(dve.memset(gate_pad[:, 0:FH], 0.0))
            fpitch = FH + TS
            pads = gate_pad[:, FH + SEQ:FPAD].rearrange("p (b c) -> p b c", b=NS)

            def ffn_tile(j, c):
                if c:
                    dve.wait_ge(f_lo_ready, j)
                dve.tensor_copy(pads[:, :, 0:FH], ffn_hist[:, :, :, bass.ds(j, 1)].rearrange("p b k a -> p b (k a)"))
                dve.wait_ge(gate_evac, j + 1)
                state = ffn_state[:, bass.ds(j, 1), :].rearrange("p a c -> p (a c)")
                dve.tensor_copy(state[:, 0:FH], gate_pad[:, SEQ:SEQ + FH])
                step(dve.tensor_copy(state[:, FH:].rearrange("p (b k) -> p b k", b=NS), pads[:, :, TS:]))
                step(dve.tensor_scalar(gate_conv[:, :], gate_pad[:, 0:FW], ffn_const[:, bass.ds(j, 1)],
                                       ffn_const[:, bass.ds(j + FCONV * FT, 1)], ALU.mult, ALU.add))
                step(dve.scalar_tensor_tensor(gate_conv[:, :], gate_pad[:, 1:1 + FW], ffn_const[:, bass.ds(j + FT, 1)],
                                              gate_conv[:, :], ALU.mult, ALU.add))
                dve.scalar_tensor_tensor(gate_conv[:, :], gate_pad[:, 2:2 + FW], ffn_const[:, bass.ds(j + 2 * FT, 1)],
                                         gate_conv[:, :], ALU.mult, ALU.add).then_inc(fconv_ready, 1)
                dve.wait_ge(val_done, j + 1)
                dve.wait_ge(gelu_ready, j + 1)
                dve.tensor_tensor(gate_pad[:, FH:FH + 2 * CW].rearrange("p (b c) -> p b c", b=2), PS[:, 3:5, 0:CW],
                                  gate_conv[:, 0:2 * CW].rearrange("p (b c) -> p b c", b=2), ALU.mult)
                dve.tensor_tensor(gate_pad[:, FH + 2 * CW:FH + SEQ], PS[:, 5, 0:SEQ - 2 * CW],
                                  gate_conv[:, 2 * CW:SEQ], ALU.mult)
                first = SEQ + FH
                dve.tensor_tensor(gate_pad[:, FH + SEQ:FH + T - TS].rearrange("p (b c) -> p b c", c=TS),
                                  PS[:, 5, SEQ - 2 * CW:CW - TS].rearrange("p (b c) -> p b c", c=TS),
                                  gate_conv[:, first:first + (NS - 1) * fpitch]
                                  .rearrange("p (b c) -> p b c", c=fpitch)[:, :, 0:TS], ALU.mult)
                dve.tensor_tensor(gate_pad[:, FH + T - TS:FH + T], PS[:, 5, CW - TS:CW],
                                  gate_conv[:, FW - TS:FW], ALU.mult).then_inc(f_ready, 1)
                dve.wait_ge(f_hi_ready, j + 1)
                subtract(f_lo[:, c, :], gate_pad[:, FH:FH + T], f_hi[:, c, :]).then_inc(f_lo_ready, 1)

            def add_output(g, q):
                dve.wait_ge(down_done, g * 18 + (q + 1))
                acc = f_acc[:, q // 2, (q % 2) * 512:(q % 2 + 1) * 512]
                dve.tensor_tensor(acc, acc, PS[:, bank_of(q), :], ALU.add).then_inc(added, 1)

            def ffn_tiles(g, more):
                for c in range(FG):
                    ffn_tile(g * FG + c, c)
                    if more:
                        for half in range(2):
                            split_group_half(g * 6 + (R_FFN + 6 + 2 * c + half), 2 * c + half)

            before = step.n
            steps_of_group = 3 * FG
            with dve.Fori(0, NG - 1) as g:
                step.base, step.n = g * steps_of_group + before, 0
                ffn_tiles(g, True)
                assert step.n == steps_of_group
                for q in range(18):
                    add_output(g, q)
                for k in range(4, 6):
                    split_group_half(g * 6 + (R_FFN + 6 + k), k)
            step.base, step.n = 0, before + (NG - 1) * steps_of_group
            ffn_tiles(NG - 1, False)

            def finish(t):
                dve.wait_ge(f_sq, t + 1)
                inv = stat[:, SS3 + t:SS3 + t + 1]
                step(dve.reciprocal(inv, inv))
                dve.scalar_tensor_tensor(f_acc[:, t, :], f_acc[:, t, :], inv, gains[:, 0, :],
                                         ALU.mult, ALU.mult).then_inc(f_normed, 1)

            dve.wait_ge(gain3_loaded, 16)
            for t in range(NT):
                add_output(NG - 1, 2 * t)
                add_output(NG - 1, 2 * t + 1)
                if t >= 1:
                    finish(t - 1)
            finish(NT - 1)

        @block.tensor
        def _(pe):
            bank_cols = lambda b, w: PS[:, b, 0:w]

            def turn(out, in_, rows=P):
                return pe.transpose(out, in_, ident[0:rows, 0:rows])

            acts = (act_hi, act_lo)

            def channels_out(banks, w, width=P, chunks=range(3)):
                for n, (wp, ap) in enumerate(((0, 0), (0, 1), (1, 0))):
                    for k in range(KD):
                        for c in chunks:
                            last = pe.matmul(PS[0:width, banks + c, 0:CW], w(wp, k),
                                             acts[ap][:, k, c * CW:(c + 1) * CW],
                                             start=(n == 0 and k == 0), stop=(n == 2 and k == KD - 1))
                return last

            pe.wait_ge(consts_ready, 2)

            def turn_x(t):
                pe.wait_ge(y_ready, t + 1)
                if t >= 2:
                    pe.wait_ge(lo_ready, t - 1)
                for k in range(KD):
                    last = turn(turned_x(t)[:, k, :], y_in[:, t % 2, k * P:(k + 1) * P])
                last.then_inc(x_turned, 1)

            def first_output(j, c, last):
                pe.wait_ge(w_lo_ready, 2)
                pe.wait_ge(lo_ready, 3 * (c + 1))
                w0 = [w[:, 0, :].rearrange("p (k c) -> p k c", k=KD) for w in (w_hi, w_lo)]
                ins = channels_out(3 * j, lambda part, k: w0[part][:, k, j * P:(j + 1) * P], chunks=[c])
                if last:
                    ins.then_inc(out_done, 1)

            for t in range(4):
                turn_x(t)
            first_output(0, 0, False)
            turn_x(4)
            turn_x(5)
            first_output(1, 0, False)
            turn_x(6)
            first_output(0, 1, False)
            turn_x(7)
            turn_x(8)
            first_output(0, 2, True)
            pe.wait_ge(lo_ready, 8)
            first_output(1, 1, False)
            pe.wait_ge(lo_ready, NT)
            pe.wait_ge(chan_loaded, 16 * 12)
            for s in range(6):
                last = turn(PS[:, 6 + s // 4, (s % 4) * P:(s % 4 + 1) * P], chan_rows[:, s, :])
            last.then_inc(chan_turned, 1)
            first_output(1, 2, True)

            seen = {0}
            w_units = [w[:, 0, :].rearrange("p (k c) -> p k c", k=KD) for w in (w_hi, w_lo)]
            for n, (kind, u, j) in enumerate(OUTS):
                if n < 2:
                    continue
                b0 = 3 * (n % 2)
                if n >= 2:
                    pe.wait_ge(out_used, n - 1)
                if u is not None and u not in seen:
                    seen.add(u)
                    pe.wait_ge(w_lo_ready, 2 * u + 2)
                    w_units = [w[:, u % 3, :].rearrange("p (k c) -> p k c", k=KD) for w in (w_hi, w_lo)]
                if kind in ("x", "y", "fq", "bq"):
                    last = channels_out(b0, lambda part, k: w_units[part][:, k, (j % 2) * P:(j % 2 + 1) * P])
                elif kind in KV:
                    for m, (ap, wp) in enumerate(((0, 0), (0, 1), (1, 0))):
                        for k in range(KD):
                            for c in range(3):
                                t = 3 * j + c
                                last = pe.matmul(bank_cols(b0 + c, DH), acts[ap][:, k, t * P:(t + 1) * P],
                                                 w_units[wp][:, k, :], start=(m == 0 and k == 0),
                                                 stop=(m == 2 and k == KD - 1))
                elif kind in ("gate_r", "gate_i"):
                    pe.wait_ge(conv_ready, j + 1)
                    pe.wait_ge(gate_w_loaded, 64)
                    for c in range(3):
                        last = pe.matmul(bank_cols(b0 + c, LW // 3), gate_w[:, int(kind == "gate_i"), j, :],
                                         xconv[:, c * (LW // 3):(c + 1) * (LW // 3)], start=True, stop=True)
                else:
                    pe.wait_ge(fa_ready, 1)
                    last = channels_out(b0, lambda part, k: (fa_hi, fa_lo)[part][:, k, :], H)
                last.then_inc(out_done, 1)
                if (kind, j) == ("fq", 0):
                    pe.wait_ge(out_used, OUTS.index(("fa", None, 0)) + 1)
                    for t in range(NT):
                        last = turn(PS[:, 6, t * H:(t + 1) * H], fa_rows[:, t * P:(t + 1) * P], H)
                    last.then_inc(fa_turned, 1)
                    for k in range(LT):
                        last = turn(PS[0:36, 7, k * P:(k + 1) * P], lru_state[:, k, :])
                    last.then_inc(state_turned, 1)
                if (kind, j) == ("fq", 1):
                    pe.wait_ge(rows_ready, 1)
                    pe.wait_ge(logf_ready, 1)
                    for t in range(NPT):
                        last = turn(PS[0:H, 6 + t // 4, (t % 4) * P:(t % 4 + 1) * P], logf[:, t, :])
                    last.then_inc(logf_turned, 1)

            def scores(n):
                st, s = STEPS[n], n % 2
                if n >= 2:
                    pe.wait_ge(scores_used, n - 1)
                if STEPS[n] in (("kf", 0), ("kb", 0)):
                    pe.wait_ge(k_loaded, 32 if st[0] == "kf" else 48)
                if n == KEY_TURNS[0]:
                    pe.wait_ge(cache_k_loaded, 32)
                if n == KEY_TURNS[NS // 2]:
                    pe.wait_ge(cache_k_loaded, 64)
                if n == FIRST["sf"]:
                    pe.wait_ge(q_blocks_ready, 1)
                if n == FIRST["sb"]:
                    pe.wait_ge(q_blocks_ready, 2)
                if st[0] == "kt":
                    cached = cache_k_low if st[1] < 2 else cache_k_high
                    for b2 in range(2):
                        for t in range(2):
                            for k in range(2):
                                c0 = (2 * t + k) * P
                                last = turn(PS[:, 2 * s + b2, c0:c0 + P],
                                            cached[:, 2 * (st[1] % 2) + b2, k, t * P:(t + 1) * P])
                elif st[0][0] == "k":
                    tiles = [(c, st[1]) for c in range(NPT)] if st[1] < 2 else [(NPT, 0), (NPT, 1)]
                    for b, (c, t) in enumerate(tiles):
                        last = turn(PS[:, 2 * s + b // 4, (b % 4) * P:(b % 4 + 1) * P],
                                    k_rows[:, c, t * P:(t + 1) * P])
                elif st[0][0] == "p":
                    h, q = st[1], st[2]
                    rows, t = slice(64 * (h % 2), 64 * (h % 2) + 64), h // 2
                    kt, tile = (kt_f, t) if st[0] == "pf" else (kt_b, 6 + t)
                    k0, nk = key_blocks(st)
                    for b in range((nk + 3) // 4):
                        n_b = min(4, nk - 4 * b)
                        c0 = (k0 + 4 * b) * P
                        diag = st[0] == "pf" and b == (nk - 1) // 4
                        last = pe.matmul(PS[:, 2 * s + b, 0:n_b * P], mix[rows, tile, q * P:(q + 1) * P],
                                         kt[rows, t, c0:c0 + n_b * P], start=True, stop=not diag)
                        if diag:
                            last = pe.matmul(PS[:, 2 * s + b, (n_b - 1) * P:n_b * P], ident_b[:, :], cmask_b[:, :],
                                             start=False, stop=True)
                else:
                    kt = kt_f if st[0] == "sf" else kt_b
                    for b2 in range(2):
                        b = 2 * st[1] + b2
                        out = PS[64 * b2:64 * b2 + 64, 2 * s, :]
                        fox = st[0] == "sf"
                        for t in range(2):
                            last = pe.matmul(out[:, 0:PAST], q_blocks[:, b, t, :], kt_s[:, b, t, :],
                                             start=t == 0, stop=(t == 1 and not fox))
                        if fox:
                            pe.matmul(out[:, 0:PAST], logf_rows[:, 2 * b, :], upper[:, 0:PAST], start=False, stop=False)
                            last = pe.matmul(out[:, P:PAST], logf_rows[:, 2 * b + 1, :], upper[:, 0:P],
                                             start=False, stop=True)
                        c0 = SEQ + TS * b
                        for t in range(2):
                            last = pe.matmul(out[:, PAST:SK], q_blocks[:, b, t, :], kt[:, t, c0:c0 + TS],
                                             start=t == 0, stop=(t == 1 and not fox))
                        if fox:
                            pe.matmul(out[:, PAST:SK], logf_rows[:, 2 * b, :], upper[:, PAST:SK], start=False, stop=False)
                            pe.matmul(out[:, PAST:SK], logf_rows[:, 2 * b + 1, :], upper[:, P:P + TS],
                                      start=False, stop=False)
                            last = pe.matmul(out[:, PAST:SK], logf_new[:, b, :], upper[:, TS * b:TS * (b + 1)],
                                             start=False, stop=True)
                last.then_inc(scores_ready, 1)

            def turn_probs(r):
                st = STEPS[REAL[r]]
                pe.wait_ge(probs_ready, r + 1)
                if r >= 1:
                    pe.wait_ge(probs_t_ready, r)
                blocks = (0, P, 512) if st[0][0] == "s" else [P * b for b in range(key_blocks(st)[1])]
                for b, c0 in enumerate(blocks):
                    last = turn(PS[:, 4 + b // 4, (b % 4) * P:(b % 4 + 1) * P], probs_of(r)[:, c0:c0 + P])
                last.then_inc(probs_turned, 1)

            def values(r):
                n = REAL[r]
                st, s = STEPS[n], r % 2
                if n == FIRST["sf"]:
                    pe.wait_ge(cache_v_loaded, 32)
                if r == 0:
                    pe.wait_ge(v_loaded[0], 16)
                if st[0] == "pf" and st[2] == 2:
                    pe.wait_ge(v_loaded[1], 32)
                if n == FIRST["pb"]:
                    pe.wait_ge(band_v_loaded, 16)
                if n == FIRST["sb"]:
                    pe.wait_ge(cache_v_loaded, 64)
                pe.wait_ge(probs_t_ready, r + 1)
                if r >= 2:
                    pe.wait_ge(att_out_used, r - 1)
                if st[0][0] == "p":
                    h = st[1]
                    v = v_f if st[0] == "pf" else v_b
                    k0, nk = key_blocks(st)
                    for b in range(nk):
                        last = pe.matmul(PS[64 * (h % 2):64 * (h % 2) + 64, 6 + s, 0:P],
                                         v[:, k0 + b, HD * h:HD * (h + 1)], probs_t[:, s, b * P:(b + 1) * P],
                                         start=b == 0, stop=b == nk - 1)
                else:
                    v = v_f if st[0] == "sf" else v_b
                    for t in range(2):
                        for b2 in range(2):
                            b = 2 * st[1] + b2
                            out = PS[:, 6 + s, (2 * t + b2) * 64:(2 * t + b2 + 1) * 64]
                            for k in range(3):
                                vals = cache_v[:, b, k, t * P:(t + 1) * P] if k < 2 else v[:, NPT, t * P:(t + 1) * P]
                                last = pe.matmul(out, vals, probs_t[:, s, k * P + 64 * b2:k * P + 64 * b2 + 64],
                                                 start=k == 0, stop=k == 2)
                last.then_inc(att_out, 1)

            pe.wait_ge(out_used, NO)
            pe.wait_ge(cum_ready, 1)
            scores(0)
            scores(1)
            scores(2)
            for n in range(NSTEP):
                if n + 3 < NSTEP:
                    scores(n + 3)
                if n in COUNT:
                    r = COUNT[n]
                    if r >= 1:
                        values(r - 1)
                    turn_probs(r)
            values(NREAL - 1)

            def turn_y2(t):
                pe.wait_ge(y2_ready, t + 1)
                if t >= 1:
                    pe.wait_ge(h2_lo, t)
                for k in range(KD):
                    last = turn(PS[:, 4 + k // 4, (k % 4) * P:(k % 4 + 1) * P], y2[:, k * P:(k + 1) * P])
                last.then_inc(y2_turned, 1)

            def wout_tile(part, h, k):
                q = 2 * h + k // 4
                w = (w_hi, w_lo)[part][:, q, :] if q < 3 else (wx_hi, wx_lo)[part][:, :]
                return w[:, (k % 4) * 512:(k % 4 + 1) * 512]

            pe.wait_ge(att_out_used, NREAL)
            pe.wait_ge(w_lo_ready, R_OUT + 4)
            for t in range(NT):
                pe.wait_ge(lo_ready, NT + t + 1)
                if t >= 2:
                    pe.wait_ge(x1_ready, t - 1)
                for h in range(2):
                    if t == 0 and h == 1:
                        pe.wait_ge(w_lo_ready, R_OUT + 8)
                    for m, (ap, wp) in enumerate(((0, 0), (0, 1), (1, 0))):
                        for k in range(KD):
                            last = pe.matmul(PS[:, mixed_banks(t) + h, :], acts[ap][:, k, t * P:(t + 1) * P],
                                             wout_tile(wp, h, k), start=(m == 0 and k == 0),
                                             stop=(m == 2 and k == KD - 1))
                    if t == NT - 1 and h == 0:
                        last.then_inc(low_half_mixed, 1)
                last.then_inc(mixed, 1)
                if t >= 1:
                    turn_y2(t - 1)

            def up_product(c, half, chunks):
                w = [x[:, c, half * 1024:(half + 1) * 1024].rearrange("p (k c) -> p k c", k=KD) for x in (w_hi, w_lo)]
                return channels_out(3 * half, lambda part, k: w[part][:, k, :], chunks=chunks)

            pe.wait_ge(h2_lo, 2 * NT // 3)
            pe.wait_ge(w_lo_ready, R_FFN + 1)
            up_product(0, 0, [0])
            up_product(0, 0, [1])
            turn_y2(NT - 1)
            pe.wait_ge(w_lo_ready, R_FFN + 2)
            up_product(0, 1, [0])
            pe.wait_ge(h2_lo, NT)
            up_product(0, 0, [2]).then_inc(gate_done, 1)
            up_product(0, 1, [1, 2]).then_inc(val_done, 1)

            def down(g, q, ks):
                t, cols = q // 2, slice((q % 2) * 512, (q % 2 + 1) * 512)
                for k in ks:
                    for m, (fp, wp) in enumerate(((0, 0), (0, 1), (1, 0))):
                        w = (w_hi, w_lo)[wp][:, 2, :].rearrange("p (k c) -> p k c", k=FG)[:, k, cols]
                        last = pe.matmul(PS[:, bank_of(q), :], (f_hi, f_lo)[fp][:, k, t * P:(t + 1) * P], w,
                                         start=(k == 0 and m == 0), stop=(k == FG - 1 and m == 2))
                if ks[-1] == FG - 1:
                    last.then_inc(down_done, 1)

            def turn_states(c):
                pe.wait_ge(added, NG * 18 + (c + 1))
                for k in range(4):
                    last = turn(PS[0:18, bank_of(8 + c), k * P:(k + 1) * P], ffn_state[:, 4 * c + k, :])
                last.then_inc(ffn_turned, 1)

            def ffn_group(g, tiles, is_last):
                for c in tiles:
                    j = g * FG + c
                    for half in range(2):
                        pe.wait_ge(w_lo_ready, g * 6 + (R_FFN + 2 * c + half + 1))
                        if c == 0:
                            pe.wait_ge(added, g * 18 + (13, 16)[half])
                        else:
                            pe.wait_ge((gate_evac, f_ready)[half], j)
                        up_product(c, half, range(3)).then_inc((gate_done, val_done)[half], 1)
                pe.wait_ge(w_lo_ready, g * 6 + (R_FFN + 6))
                pe.wait_ge(f_lo_ready, g * FG + 1)
                pe.wait_ge(added, g * 18 + 18)
                for q in range(8):
                    if q == 2:
                        pe.wait_ge(gate_evac, g * FG + FG)
                    if q == 5:
                        pe.wait_ge(f_ready, g * FG + FG)
                    down(g, q, [0])
                pe.wait_ge(f_lo_ready, g * FG + FG)
                for q in range(8):
                    if is_last and q == 7:
                        turn_states(0)
                    down(g, q, [1])
                for q in range(8, 18):
                    if is_last and q - 7 < 6:
                        turn_states(q - 7)
                    if is_last and q - 8 < 6:
                        pe.wait_ge(ffn_rows_ready, q - 7)
                    pe.wait_ge(added, g * 18 + (18 + q - 7))
                    down(g, q, [0, 1])

            ffn_group(0, range(1, FG), False)
            with pe.Fori(1, NG - 1) as g:
                ffn_group(g, range(FG), False)
            ffn_group(NG - 1, range(FG), True)


_NAMES = ["x_prompt", "x_sample", "cache_fox_k", "cache_fox_v", "cache_fox_logf", "cache_band_k", "cache_band_v",
          "state_lru_h", "state_lru_conv", "state_ffn_conv", "norm_g", "w_in", "b_forget", "lru_conv_w", "lru_conv_b",
          "lru_wa", "lru_ba", "lru_wx", "lru_bx", "lru_lambda", "rel_bias", "w_out", "w_up", "ffn_conv_w",
          "ffn_conv_b", "w_down"]
_KEEP = CHUNK * 8
_OUTPUTS = [("y_prompt", (1, SEQ, D)), ("y_sample", (NS, TS, D)),
            ("fox_k_p", (1, 1, SEQ, H, HD)), ("fox_k_s", (1, NS, TS, H, HD)),
            ("fox_v_p", (1, 1, SEQ, H, HD)), ("fox_v_s", (1, NS, TS, H, HD)),
            ("fox_logf_p", (1, 1, SEQ, H)), ("fox_logf_s", (1, NS, TS, H)),
            ("band_k_p", (1, 1, _KEEP, H, HD)), ("band_k_s", (1, NS, TS, H, HD)),
            ("band_v_p", (1, 1, _KEEP, H, HD)), ("band_v_s", (1, NS, TS, H, HD)),
            ("lru_h_p", (1, 1, DL)), ("lru_h_s", (1, NS, DL)),
            ("lru_conv_p", (1, 1, LH, DL)), ("lru_conv_s", (1, NS, LH, DL)),
            ("ffn_conv_p", (1, 1, FH, DFF)), ("ffn_conv_s", (1, NS, FH, DFF))]


def kernel(**inputs):
    import numpy as np
    import concourse.bacc as bacc
    from concourse.bass_utils import run_bass_kernel_spmd

    nc = bacc.Bacc("TRN2", target_bir_lowering=False, num_devices=1)
    arrays, ins, outs = {}, {}, {}
    for name in _NAMES:
        a = np.ascontiguousarray(inputs[name])
        arrays[f"in_{name}"] = a
        ins[name] = nc.dram_tensor(f"in_{name}", a.shape, mybir.dt.from_np(a.dtype), kind="ExternalInput").ap()
    for name, shape in _OUTPUTS:
        outs[name] = nc.dram_tensor(f"out_{name}", shape, F32, kind="ExternalOutput").ap()
    encoder_step(nc, ins, outs)
    r = run_bass_kernel_spmd(nc, [arrays], core_ids=[0])
    return tuple(r.results[0][f"out_{name}"] for name, _ in _OUTPUTS)
```
